# Optimizing a Trainium2 kernel written in Bass

```python
import jax, jax.numpy as jnp
from jax import lax
import numpy as np

D_MODEL = 1024
BATCH = 1
SEQ = 1024
DEPTH = 1

CHUNK = 64
MIX_WIDTH = D_MODEL
CONV_WIDTH = MIX_WIDTH // 2
CONV_KERNEL = 31
HGRN_WIDTH = MIX_WIDTH - CONV_WIDTH
HGRN_HEAD_DIM = 128
HGRN_HEADS = HGRN_WIDTH // HGRN_HEAD_DIM
IN_WIDTH = 2 * CONV_WIDTH + 4 * HGRN_WIDTH
D_FF = -(-8 * D_MODEL // (3 * 256)) * 256
N_MOD = 6
EPS = 1e-6

kernel_name = "hymba_conformer_hgrn2_adaln_block"

def rms_norm(x, g):
    xf = x.astype(jnp.float32)
    y = xf * lax.rsqrt(jnp.mean(xf * xf, axis=-1, keepdims=True) + EPS)
    return (y * g.astype(jnp.float32)).astype(x.dtype)

def layer_norm(x, g, b):
    xf = x.astype(jnp.float32)
    mu = jnp.mean(xf, axis=-1, keepdims=True)
    var = jnp.mean(jnp.square(xf - mu), axis=-1, keepdims=True)
    y = (xf - mu) * lax.rsqrt(var + EPS)
    return (y * g.astype(jnp.float32) + b.astype(jnp.float32)).astype(x.dtype)

def conformer_conv(val, gate, w, b, ln_g, ln_b):
    u = val * jax.nn.sigmoid(gate)
    y = lax.conv_general_dilated(
        u, w[:, None, :].astype(u.dtype), window_strides=(1,),
        padding=[(CONV_KERNEL - 1, 0)],
        dimension_numbers=('NWC', 'WIO', 'NWC'),
        feature_group_count=u.shape[-1]) + b.astype(u.dtype)
    return jax.nn.silu(layer_norm(y, ln_g, ln_b))

def hgrn2(q_raw, f_raw, i_raw, g_raw, lb, norm_g):
    B, S, _ = q_raw.shape
    n_chunks = S // CHUNK
    f32 = jnp.float32
    q = jax.nn.silu(q_raw.astype(f32))
    z = f_raw.astype(f32)
    lb = lb.astype(f32)
    log_f = jnp.logaddexp(jnp.log(lb), jnp.log1p(-lb) + jax.nn.log_sigmoid(z))
    k = (1.0 - lb) * jax.nn.sigmoid(-z)
    v = i_raw.astype(f32)

    def to_chunks(t):
        return t.reshape(B, n_chunks, CHUNK, HGRN_HEADS, HGRN_HEAD_DIM).transpose(1, 0, 3, 2, 4)

    qc, kc, vc = to_chunks(q), to_chunks(k), to_chunks(v)
    bc = jnp.cumsum(to_chunks(log_f), axis=3)
    mask = jnp.tril(jnp.ones((CHUNK, CHUNK), dtype=bool))[:, :, None]

    def step(state, inp):
        q_, k_, v_, b_ = inp
        rel = jnp.where(mask, b_[:, :, :, None, :] - b_[:, :, None, :, :], -jnp.inf)
        scores = jnp.einsum('bhtsk,bhsk->bhts', jnp.exp(rel) * q_[:, :, :, None, :], k_)
        o = (jnp.einsum('bhts,bhsv->bhtv', scores, v_)
             + jnp.einsum('bhtk,bhkv->bhtv', q_ * jnp.exp(b_), state))
        b_end = b_[:, :, -1:, :]
        state = (jnp.exp(b_end[:, :, 0, :])[..., None] * state
                 + jnp.einsum('bhsk,bhsv->bhkv', k_ * jnp.exp(b_end - b_), v_))
        return state, o

    s0 = jnp.zeros((B, HGRN_HEADS, HGRN_HEAD_DIM, HGRN_HEAD_DIM), f32)
    _, o = lax.scan(step, s0, (qc, kc, vc, bc))
    o = o.transpose(1, 0, 3, 2, 4).reshape(B, S, HGRN_HEADS, HGRN_HEAD_DIM)
    o = rms_norm(o, norm_g).reshape(B, S, HGRN_WIDTH)
    return (o * jax.nn.silu(g_raw.astype(f32))).astype(q_raw.dtype)

def setup_inputs(seed: int = 0) -> dict:
    key = jax.random.key(seed)
    ks = jax.random.split(key, 20)
    nrm = lambda k, shape, s: jax.random.normal(k, shape, jnp.float32) * s
    gain = lambda k, shape: 1.0 + nrm(k, shape, 0.05)
    return {
        "x": nrm(ks[0], (BATCH, SEQ, D_MODEL), 1.0),
        "c": nrm(ks[1], (BATCH, D_MODEL), 1.0),
        "w_ada": nrm(ks[2], (DEPTH, D_MODEL, N_MOD * D_MODEL), D_MODEL ** -0.5),
        "b_ada": nrm(ks[3], (DEPTH, N_MOD * D_MODEL), 0.02),
        "g_pre_mix": gain(ks[4], (DEPTH, D_MODEL)),
        "g_post_mix": gain(ks[5], (DEPTH, D_MODEL)),
        "w_in": nrm(ks[6], (DEPTH, D_MODEL, IN_WIDTH), D_MODEL ** -0.5),
        "conv_w": nrm(ks[7], (DEPTH, CONV_KERNEL, CONV_WIDTH), CONV_KERNEL ** -0.5),
        "conv_b": nrm(ks[8], (DEPTH, CONV_WIDTH), 0.02),
        "conv_ln_g": gain(ks[9], (DEPTH, CONV_WIDTH)),
        "conv_ln_b": nrm(ks[10], (DEPTH, CONV_WIDTH), 0.02),
        "hgrn_lower_bounds": nrm(ks[11], (DEPTH, HGRN_WIDTH), 0.1),
        "hgrn_norm_g": gain(ks[12], (DEPTH, HGRN_HEAD_DIM)),
        "w_out": nrm(ks[13], (DEPTH, MIX_WIDTH, D_MODEL), MIX_WIDTH ** -0.5),
        "g_pre_ffn": gain(ks[14], (DEPTH, D_MODEL)),
        "g_post_ffn": gain(ks[15], (DEPTH, D_MODEL)),
        "w_ffn_in": nrm(ks[16], (DEPTH, D_MODEL, 2 * D_FF), D_MODEL ** -0.5),
        "w_ffn_out": nrm(ks[17], (DEPTH, D_FF, D_MODEL), D_FF ** -0.5),
    }

def reference(x, c, w_ada, b_ada, g_pre_mix, g_post_mix, w_in, conv_w, conv_b,
              conv_ln_g, conv_ln_b, hgrn_lower_bounds, hgrn_norm_g, w_out,
              g_pre_ffn, g_post_ffn, w_ffn_in, w_ffn_out):
    lb_all = jnp.cumsum(jax.nn.softmax(hgrn_lower_bounds.astype(jnp.float32), axis=0), axis=0)
    lb_all = lb_all - lb_all[0:1]
    cond = jax.nn.silu(c)
    splits = [CONV_WIDTH, 2 * CONV_WIDTH,
              2 * CONV_WIDTH + HGRN_WIDTH,
              2 * CONV_WIDTH + 2 * HGRN_WIDTH,
              2 * CONV_WIDTH + 3 * HGRN_WIDTH]
    for l in range(DEPTH):
        mod = cond @ w_ada[l] + b_ada[l]
        sh1, sc1, gt1, sh2, sc2, gt2 = [m[:, None, :] for m in jnp.split(mod, N_MOD, axis=-1)]

        h = rms_norm(x, g_pre_mix[l]) * (1.0 + sc1) + sh1
        zin = h @ w_in[l]
        cv_val, cv_gate, q, f, i, og = jnp.split(zin, splits, axis=-1)
        out_a = conformer_conv(cv_val, cv_gate, conv_w[l], conv_b[l], conv_ln_g[l], conv_ln_b[l])
        out_b = hgrn2(q, f, i, og, lb_all[l], hgrn_norm_g[l])
        mix = jnp.concatenate([out_a, out_b], axis=-1) @ w_out[l]
        x = x + gt1 * rms_norm(mix, g_post_mix[l])

        h2 = rms_norm(x, g_pre_ffn[l]) * (1.0 + sc2) + sh2
        gate, up = jnp.split(h2 @ w_ffn_in[l], 2, axis=-1)
        y = (jax.nn.silu(gate) * up) @ w_ffn_out[l]
        x = x + gt2 * rms_norm(y, g_post_ffn[l])
    return x


_drawn_inputs = setup_inputs


def setup_inputs(seed=0):
    import zlib

    import numpy as np

    out = dict(_drawn_inputs(seed))
    spreads = {}
    factors = {'conv_b': 6.503, 'conv_ln_g': 2.985, 'conv_ln_b': 8.0, 'hgrn_norm_g': 3.073}
    for name, (base, spread) in spreads.items():
        noise = np.random.default_rng([zlib.crc32(name.encode()), seed]).standard_normal(out[name].shape)
        drawn = base * np.exp(spread * noise) if base else spread * noise
        out[name] = __import__('jax').numpy.asarray(drawn.astype(out[name].dtype))
    for name, factor in factors.items():
        out[name] = (out[name] * factor).astype(out[name].dtype)
    return out
```

```python
from contextlib import ExitStack

import concourse.bass as bass
from concourse import mybir

F32 = mybir.dt.float32
F32R = mybir.dt.float32r
BF16 = mybir.dt.bfloat16
I32 = mybir.dt.int32
ALU = mybir.AluOpType
ACT = mybir.ActivationFunctionType
AX_X = mybir.AxisListType.X
ds = bass.ds

P = 128
D = 1024
S = 1024
KT = D // P
TT = S // P
HALF = 512
CHUNK = 64
TAPS = 31
HEADS = 4
CT = 4
FFT = 22
FB = FFT // 2
D_FF = FFT * P
EPS = 1e-6
LEVELS = [64, 32, 16, 8, 4, 2]

RAW = 2
WS = 3
N_IN = 6 * 4
N_OUT = KT
N_FFN = 3 * FFT
N_CHUNKS = N_IN + N_OUT + N_FFN

ROW_C, ROW_GPRE1, ROW_GPOST1, ROW_GPRE2, ROW_GPOST2 = 0, 8, 16, 24, 32
ROW_BADA, ROW_CB, ROW_LNG, ROW_LNB, ROW_LB, ROW_NG, ROWS = 40, 88, 92, 96, 100, 104, 105


AT_DVE = ["DKD", "D0", "KD", "QE", "D1", "XL0", "X0", "D2", "XL1", "X1", "PD", "P0", "D3", "XL2", "X2", "P1",
          "D4", "XL3", "X3", "P2", "D5", "XL4", "X4", "P3", "XL5", "X5", "P4", "ST1", "ST1", "ST1", "ST1", "P5",
          "SS", "ST0", "ST0", "ST0", "ST0", "ON", "MIX", "LO"]
AT_ACT = ["KC", "VC", "EKD", "EB", "EL0", "E0", "EL1", "E1", "EL2", "E2", "KDT", "EL3", "E3", "EL4", "E4",
          "EL5", "E5", "SQ", "LN", "RSTD", "HI"]
AT_PE = ["KDT", "DIAG", "S0", "S1", "S2", "S3", "S4", "S5", "C0", "C1", "O", "OT"]
AT_DVE0 = 2
VEC_LOADS = 12
CREDIT = 1
LN_DVE = 3 * CT


class Tally:

    def __init__(self, eng, sem):
        self.eng, self.sem, self.base, self.turn, self.per, self.n = eng, sem, 0, 0, 0, 0

    def done(self, instruction):
        instruction.then_inc(self.sem, 1)
        self.n += 1

    def wait(self, behind=0):
        self.eng.wait_ge(self.sem, self.base + self.turn * self.per + self.n - behind)

    def last(self):
        return self.sem, self.base + self.turn * self.per + self.n

    def enter(self, turn, per):
        self.base, self.turn, self.per, self.n = self.base + self.n, turn, per, 0

    def leave(self, turns):
        assert self.n == self.per, (self.n, self.per)
        self.base, self.turn, self.per, self.n = self.base + self.per * turns, 0, 0, 0


def build(nc, t_in, out):
    x_d = t_in["x"].rearrange("a (i p) d -> (a p) i d", p=P)
    out_d = out.rearrange("a (i p) d -> (a p) i d", p=P)
    w_ada_d = t_in["w_ada"].rearrange("l (kt p) n -> (l p) kt n", p=P)
    w_in_d = t_in["w_in"].rearrange("l (kt p) n -> (l p) kt n", p=P)
    w_out_d = t_in["w_out"].rearrange("l (kt p) n -> (l p) kt n", p=P)
    w_up_d = t_in["w_ffn_in"].rearrange("l (kt p) n -> (l p) kt n", p=P)
    w_down_d = t_in["w_ffn_out"].rearrange("l (f p) n -> (l p) f n", p=P)
    y_spill = nc.dram_tensor("conv_spill", [P, CT, S], F32).ap()
    og_spill = nc.dram_tensor("og_spill", [P, HEADS, S], F32).ap()

    ctx = ExitStack()
    with ctx:
        def sem(name):
            return ctx.enter_context(nc.semaphore(name))

        def group(specs):
            made = []
            with ExitStack() as place:
                for name, shape, dt in specs:
                    made.append(place.enter_context(nc.sbuf_tensor(name, shape, dt)))
            return made

        def keep(name, shape, dt=F32):
            return ctx.enter_context(nc.sbuf_tensor(name, shape, dt))

        ident = keep("ident", [P, P])
        ones = keep("ones", [P, P])
        masks = keep("masks", [P, len(LEVELS), P])
        scan_keep = keep("scan_keep", [P, S], BF16)
        rows_a = keep("rows_a", [ROWS, P])
        rows_b = keep("rows_b", [TAPS * CT, P])
        vec = keep("vec", [P, ROWS])
        conv_w_col = keep("conv_w_col", [P, TAPS * CT])
        mod = keep("mod", [P, 48])
        cond = keep("cond", [P, KT])
        gs = keep("gs", [P, 2, KT])
        gg = keep("gg", [P, 2, KT])
        lb_tmp = keep("lb_tmp", [P, 5, HEADS])
        one_less_lb = keep("one_less_lb", [P, HEADS])
        log_one_less_lb = keep("log_one_less_lb", [P, HEADS])
        tile_w = keep("tile_w", [P, TAPS])
        tile_cols = keep("tile_cols", [P, 3])
        ss = keep("ss", [P, 4, TT])
        rs = keep("rs", [P, 4, TT])
        ggb = keep("ggb", [P, D])
        raw = keep("raw", [P, RAW, D])
        w_hi = keep("w_hi", [P, WS, D], F32R)
        w_lo = keep("w_lo", [P, WS, D], F32R)

        w2k = [P, HEADS, P]
        xr, dd, ee, qe, kd, kc, kdt, vc, sq, on = group([
            ("xr", [P, 3, HEADS, P], F32), ("dd", [P, 2, HEADS, P], F32), ("ee", [P, 2, HEADS, P], F32),
            ("qe", w2k, F32), ("kd", w2k, F32), ("kc", w2k, F32), ("kdt", w2k, F32), ("vc", w2k, F32),
            ("sq", w2k, F32), ("on", w2k, F32)])
        ha_hi = keep("ha_hi", [P, 4, S], F32R)
        ha_lo = keep("ha_lo", [P, 4, S], F32R)
        hb_hi = keep("hb_hi", [P, 4, S], F32R)
        hb_lo = keep("hb_lo", [P, 4, S], F32R)

        x0, ada0, acc0, _, full0 = group([("x0", [P, TT, D], F32), ("ada0", [P, 3, 2 * D], F32),
                                          ("acc0", [P, 2 * D], F32), ("pad0", [P, 16], F32),
                                          ("full0", [P, 2, HALF], F32)])
        q, k, b, v, u, y, ogt, vt, ada, acc = group([
            ("q", [P, HEADS, S], F32), ("k", [P, HEADS, S], F32), ("b", [P, HEADS, S], F32),
            ("v", [P, TT, HEADS * P], F32), ("u", [P, S + TAPS - 1], F32), ("y", [P, S], F32),
            ("ogt", [P, S], F32), ("vt", [P, S], F32), ("ada", [P, 2, D], F32), ("acc", [P, D], F32)])
        _, pmat, state, ogc, mixf, eb = group([
            ("qkbv", [P, 4 * HEADS * S], F32), ("pmat", w2k, F32), ("state", [P, 2, HEADS, P], F32),
            ("ogc", [P, 2, HEADS, P], F32), ("mixf", w2k, F32), ("eb", w2k, F32)])
        y4, ln_sq, ln_rs, ln_f = group([("y4", [P, CT, S], F32), ("ln_sq", [P, 2, S], F32),
                                        ("ln_rs", [P, S], F32), ("ln_f", [P, 2, S], F32)])
        mt, x1, xs = group([("mt", [P, KT, S], F32), ("x1", [P, TT, D], F32), ("xs", [P, TT, D], F32)])
        full1, = group([("full1", [P, 2, HALF], F32)])
        _, _, gate, ufull, u_hi, u_lo = group([
            ("yt_", [P, KT, S], F32), ("x1_", [P, TT, D], F32), ("gate", [P, S], F32),
            ("ufull", [P, S], F32), ("u_hi", [P, 2, S], F32R), ("u_lo", [P, 2, S], F32R)])
        _, _, tail_tmp = group([("yt__", [P, KT, S], F32), ("x1__", [P, TT, D], F32),
                                ("tail_tmp", [P, 2, D], F32)])
        pair = [ctx.enter_context(nc.psum_tensor(f"pair{i}", [P, S], F32)) for i in range(4)]

        def bank(i):
            return pair[i // 2][:, (i % 2) * HALF:(i % 2 + 1) * HALF]

        consts_ready = sem("consts_ready")
        vec_loaded = sem("vec_loaded")
        vec_turned = sem("vec_turned")
        vec_ready = sem("vec_ready")
        cond_ready = sem("cond_ready")
        x_loaded = [sem(f"x_loaded{i}") for i in range(2)]
        x1_loaded = sem("x1_loaded")
        ada0_loaded = [sem(f"ada0_loaded{i}") for i in range(3)]
        ada0_used = sem("ada0_used")
        acc0_ready = sem("acc0_ready")
        mod0_summed = sem("mod0_summed")
        mod_ready = sem("mod_ready")
        ss_ready = sem("ss_ready")
        xs_ready = sem("xs_ready")
        turned = sem("turned")
        full_ready = sem("full_ready")
        hi_ready = sem("hi_ready")
        h_ready = sem("h_ready")
        raw_loaded = [sem(f"raw_loaded{i}") for i in range(RAW)]
        w_split = sem("w_split")
        w_used = sem("w_used")
        gate_sig = sem("gate_sig")
        q_evac = sem("q_evac")
        og_evac = sem("og_evac")
        vt_evac = sem("vt_evac")
        z_evac = sem("z_evac")
        u_evac = sem("u_evac")
        ada_loaded = [sem(f"ada_loaded{i}") for i in range(2)]
        ada_used = sem("ada_used")
        modt_summed = sem("modt_summed")
        modt_ready = sem("modt_ready")
        z_log = sem("z_log")
        tap_done = sem("tap_done")
        y_stored = sem("y_stored")
        og_stored = sem("og_stored")
        v_turned = sem("v_turned")
        v_ready = sem("v_ready")
        act_self = sem("act_self")
        dve_self = sem("dve_self")
        pool_self = sem("pool_self")
        at_act = sem("at_act")
        at_dve = sem("at_dve")
        at_pe = sem("at_pe")
        ogc_loaded = [sem(f"ogc_loaded{i}") for i in range(2)]
        y4_loaded = sem("y4_loaded")
        ln_pe = sem("ln_pe")
        ln_dve = sem("ln_dve")
        ln_act = sem("ln_act")
        mt_ready = sem("mt_ready")
        ggb_pe = sem("ggb_pe")
        ggb_ready = sem("ggb_ready")
        tail_turned = sem("tail_turned")
        tail_ss = sem("tail_ss")
        tail_done = sem("tail_done")
        x1_ss = sem("x1_ss")
        gate_silu = sem("gate_silu")
        ufull_ready = sem("ufull_ready")
        uhi_ready = sem("uhi_ready")
        u_ready = sem("u_ready")
        down_ready = sem("down_ready")
        y_added = sem("y_added")
        yt_zero = sem("yt_zero")
        out_stored = sem("out_stored")

        def after(order, turn, name, before=0):
            return turn * len(order) + (before + len(order) - order[::-1].index(name))

        passed = sem("passed")

        def apart(eng, *waits):
            for s_, n in waits:
                eng.wait_ge(s_, n)
            eng.sem_inc(passed, 1)

        block = ctx.enter_context(nc.Block())

        @block.sync
        def _(sp):
            a = lambda t, n: t.rearrange("l (r c) -> (l r) c", c=P)
            for row, name, n in ((ROW_C, "c", 8), (ROW_GPRE1, "g_pre_mix", 8), (ROW_GPOST1, "g_post_mix", 8),
                                 (ROW_GPRE2, "g_pre_ffn", 8), (ROW_GPOST2, "g_post_ffn", 8),
                                 (ROW_BADA, "b_ada", 48), (ROW_CB, "conv_b", 4), (ROW_LNG, "conv_ln_g", 4),
                                 (ROW_LNB, "conv_ln_b", 4), (ROW_LB, "hgrn_lower_bounds", 4),
                                 (ROW_NG, "hgrn_norm_g", 1)):
                sp.dma_start(rows_a[row:row + n, :], a(t_in[name], n)).then_inc(vec_loaded, 16)
            sp.dma_start(rows_b[:, :], t_in["conv_w"].rearrange("l j (t c) -> (l j t) c", c=P)).then_inc(vec_loaded, 16)
            for i in range(2):
                sp.dma_start(x0[:, 4 * i:4 * i + 4, :], x_d[:, 4 * i:4 * i + 4, :]).then_inc(x_loaded[i], 16)

            def load(g, src, ready):
                if ready is not None:
                    apart(sp, (w_split, ready))
                sp.dma_start(raw[:, g % RAW, :] if src.shape[1] != KT else
                             raw[:, g % RAW, :].rearrange("p (kt c) -> p kt c", kt=KT), src
                             ).then_inc(raw_loaded[g % RAW], 16)

            def in_tile(base, t):
                return w_in_d[:, :, ds(t * P + base * P, P)]

            def in_round(t, first):
                for j, base in enumerate((4, 0, 12, 8, 20, 16)):
                    load(j, in_tile(base, t), None if first and j < RAW else t * 6 + (j - 1))
            in_round(0, True)
            with sp.Fori(1, 4) as t:
                in_round(t, False)
            ahead = RAW + WS
            for n in range(ahead):
                load(N_IN + n, w_out_d[:, :, n * P:(n + 1) * P], N_IN + n - 1)
            sp.wait_ge(og_stored, 16 * HEADS + 16 * CREDIT)
            sp.wait_ge(y_stored, 16 * CT + 16 * CREDIT)
            sp.wait_ge(v_ready, HEADS + CREDIT)
            for par in range(2):
                sp.dma_start(ogc[:, par], og_spill[:, :, par * P:(par + 1) * P]).then_inc(ogc_loaded[par], 16)
            with sp.Fori(2, TT - 1, 2) as c:
                for par in range(2):
                    apart(sp, (at_dve, after(AT_DVE, c + (par - 2), "MIX", AT_DVE0)))
                    sp.dma_start(ogc[:, par], og_spill[:, :, ds(c * P + par * P, P)]).then_inc(ogc_loaded[par], 16)
            sp.wait_ge(at_dve, after(AT_DVE, TT - 1, "LO", AT_DVE0))
            sp.dma_start(y4[:, :, :], y_spill).then_inc(y4_loaded, 16)
            sp.wait_ge(ln_dve, LN_DVE)
            sp.dma_start(x1[:, :, :], x_d).then_inc(x1_loaded, 16)
            for n in range(ahead, N_OUT):
                load(N_IN + n, w_out_d[:, :, n * P:(n + 1) * P], N_IN + n - 1)

            G0 = N_IN + N_OUT
            load(G0, w_up_d[:, :, 0:P], G0 - 1)
            load(G0 + 1, w_up_d[:, :, D_FF:D_FF + P], G0)

            def ffn_round(bk, last):
                g = G0 + 2
                srcs = [w_up_d[:, :, ds(bk * 2 * P + P, P)], w_up_d[:, :, ds(bk * 2 * P + P + D_FF, P)]]
                if not last:
                    srcs += [w_up_d[:, :, ds(bk * 2 * P + 2 * P, P)], w_up_d[:, :, ds(bk * 2 * P + 2 * P + D_FF, P)]]
                srcs += [w_down_d[:, ds(bk * 2, 1), :], w_down_d[:, ds(bk * 2 + 1, 1), :]]
                for j, src in enumerate(srcs):
                    load(g + j, src, bk * 6 + (g + j - 1))
            with sp.Fori(0, FB - 1) as bk:
                ffn_round(bk, False)
            ffn_round(FB - 1, True)
            for i in range(TT):
                sp.wait_ge(tail_done, TT + i + 1)
                sp.dma_start(out_d[:, i, :], x1[:, i, :]).then_inc(out_stored, 16)
            sp.wait_ge(out_stored, 16 * TT)

        @block.gpsimd
        def _(pool):
            me = Tally(pool, pool_self)
            me.done(pool.memset(ident[:, :], 0.0))
            pool.memset(ones[:, :], 1.0).then_inc(consts_ready, 1)
            me.done(pool.memset(masks[:, :, :], 1.0))
            me.wait()
            pool.affine_select(out=ident[:, :], in_=ident[:, :], compare_op=ALU.not_equal, fill=1.0, base=0,
                               pattern=[[-1, P]], channel_multiplier=1).then_inc(consts_ready, 1)
            for n, size in enumerate(LEVELS):
                half, blocks = size // 2, P // size
                m = masks[:, n, :].rearrange("s (b h c) -> s b h c", h=2, c=half)
                me.done(pool.memset(m[:, :, 0, :], 0.0))
                right = m[:, :, 1, :]
                me.done(pool.affine_select(out=right, in_=right, compare_op=ALU.is_ge, fill=0.0, base=0,
                                           pattern=[[-size, blocks], [0, half]], channel_multiplier=1))
                me.wait()
                me.done(pool.affine_select(out=right, in_=right, compare_op=ALU.is_ge, fill=0.0, base=half - 1,
                                           pattern=[[size, blocks], [0, half]], channel_multiplier=-1))
            me.wait()
            pool.memset(lb_tmp[:, 4, :], 0.0).then_inc(consts_ready, 1)

            def split(j, loads, free):
                apart(pool, (raw_loaded[j % RAW], loads), *([(w_used, free)] if free is not None else []))
                hi, lo, src = w_hi[:, j % WS, :], w_lo[:, j % WS, :], raw[:, j % RAW, :]
                me.done(pool.tensor_copy(hi, src))
                me.wait()
                pool.tensor_tensor(lo, src, hi, ALU.subtract).then_inc(w_split, 1)

            for j in range(6):
                split(j, 16 * (j // RAW + 1), None if j < WS else j - WS + 1)
            turns = N_CHUNKS // 6 - 1
            with pool.Fori(1, turns + 1) as r:
                me.enter(r + (-1), 6)
                for j in range(6):
                    split(j, r * 16 * (6 // RAW) + 16 * (j // RAW + 1), r * 6 + (j - WS + 1))
            me.leave(turns)
            for j in range(N_CHUNKS % 6):
                g = 6 * (turns + 1) + j
                split(j, 16 * (g // RAW + 1), g - WS + 1)

        @block.scalar
        def _(act):
            me = Tally(act, act_self)
            for s_ in (og_evac, vt_evac, v_ready):
                act.sem_inc(s_, CREDIT)
            for s_ in (og_stored, y_stored):
                act.sem_inc(s_, 16 * CREDIT)

            def root_mean_square(src, junk, col, which, count):
                me.done(act.activation(junk, src, ACT.Square, accum_out=ss[:, which, col:col + 1]))
                me.wait()
                return act.activation(rs[:, which, col:col + 1], ss[:, which, col:col + 1], ACT.Sqrt,
                                      scale=1.0 / count, bias=EPS)

            act.wait_ge(vec_ready, 2)
            act.activation(cond[:, :], vec[:, ROW_C:ROW_C + KT], ACT.Silu).then_inc(cond_ready, 1)
            for kt in range(3):
                act.dma_start(ada0[:, kt, :], w_ada_d[:, kt, 0:2 * D]).then_inc(ada0_loaded[kt], 16)
            act.activation(lb_tmp[:, 1, :], lb_tmp[:, 0, :], ACT.Exp).then_inc(cond_ready, 1)
            act.wait_ge(vec_ready, 3)
            act.activation(log_one_less_lb[:, :], one_less_lb[:, :], ACT.Ln).then_inc(cond_ready, 1)
            for i in range(TT):
                act.wait_ge(x_loaded[i // 4], 16)
                root_mean_square(x0[:, i, :], pair[2][:, :], i, 0, D).then_inc(ss_ready, 1)
            for kt in range(3, KT):
                act.wait_ge(ada0_used, kt - 2)
                act.dma_start(ada0[:, kt % 3, :], w_ada_d[:, kt, 0:2 * D]).then_inc(ada0_loaded[kt % 3], 16)

            def hi_parts(call, full):
                for g in range(16):
                    kt, half = g // 2, g % 2
                    act.wait_ge(full_ready, 16 * call + g + 1)
                    dst = (ha_hi if kt < 4 else hb_hi)[:, kt % 4, half * HALF:(half + 1) * HALF]
                    act.activation(dst, full[:, g % 2, :], ACT.Copy).then_inc(hi_ready, 1)
            hi_parts(0, full0)

            act.wait_ge(h_ready, 16)
            with act.Fori(0, 4) as t:
                me.enter(t, 3)
                for j in range(KT):
                    act.wait_ge(ada_used, t * KT + max(0, j - 1) + CREDIT)
                    act.dma_start(ada[:, j % 2, :], w_ada_d[:, j, ds(t * D + 2 * D, D)]).then_inc(ada_loaded[j % 2], 16)
                act.wait_ge(w_used, t * 6 + 1)
                act.wait_ge(tap_done, t * 2 * TAPS + CREDIT)
                act.activation(u[:, TAPS - 1:], pair[0][:, :], ACT.Sigmoid).then_inc(gate_sig, 1)
                apart(act, (w_used, t * 6 + 3))
                me.done(act.activation(k[:, t, :], pair[0][:, :], ACT.Sigmoid, scale=-1.0))
                me.done(act.activation(b[:, t, :], pair[0][:, :], ACT.Abs))
                apart(act, me.last())
                me.done(act.activation(b[:, t, :], b[:, t, :], ACT.Exp, scale=-1.0))
                apart(act, me.last())
                act.activation(b[:, t, :], b[:, t, :], ACT.Ln, bias=1.0).then_inc(z_log, 1)
                apart(act, (w_used, t * 6 + 4))
                act.activation(q[:, t, :], pair[1][:, :], ACT.Silu).then_inc(q_evac, 1)
                act.wait_ge(w_used, t * 6 + 5)
                act.wait_ge(og_stored, t * 16 + 16 * CREDIT)
                act.activation(ogt[:, :], pair[0][:, :], ACT.Silu).then_inc(og_evac, 1)
                act.wait_ge(og_evac, t + 1 + CREDIT)
                act.dma_start(og_spill[:, t, :], ogt[:, :]).then_inc(og_stored, 16)
                act.wait_ge(w_used, t * 6 + 6)
                act.activation(vt[:, :], pair[1][:, :], ACT.Copy).then_inc(vt_evac, 1)
                apart(act, (v_turned, t + 1))
                act.activation(v[:, :, ds(t * P, P)], pair[2][:, :].rearrange("s (c n) -> s c n", n=P),
                               ACT.Copy).then_inc(v_ready, 1)
                act.wait_ge(tap_done, t * 2 * TAPS + 2 * TAPS + CREDIT)
                act.dma_start(y_spill[:, t, :], y[:, :]).then_inc(y_stored, 16)
            me.leave(4)

            act.wait_ge(at_dve, AT_DVE0)
            act.wait_ge(v_ready, HEADS + CREDIT)
            with act.Fori(0, TT) as c:
                order = []

                def signal(name, i_):
                    i_.then_inc(at_act, 1)
                    order.append(name)

                def dve_done(name):
                    act.wait_ge(at_dve, after(AT_DVE, c, name, AT_DVE0))
                cols = ds(c * P, P)
                signal("KC", act.activation(kc[:, :, :], k[:, :, cols], ACT.Copy))
                signal("VC", act.activation(vc[:, :, :], v[:, c, :].rearrange("s (h n) -> s h n", n=P), ACT.Copy))
                dve_done("DKD")
                signal("EKD", act.activation(ee[:, 1], dd[:, 1], ACT.Exp, scale=-1.0))
                signal("EB", act.activation(eb[:, :, :], b[:, :, cols], ACT.Exp))
                for n, size in enumerate(LEVELS):
                    dve_done(f"D{n}")
                    if n == 3:
                        act.wait_ge(at_pe, after(AT_PE, c, "KDT"))
                        signal("KDT", act.activation(kdt[:, :, :], bank(2).rearrange("s (h n) -> s h n", n=P), ACT.Copy))
                    dv, ev = (w[:, n % 2].rearrange("p h (g s c) -> p (h g) s c", s=2, c=size // 2) for w in (dd, ee))
                    signal(f"EL{n}", act.activation(ev[:, :, 0, :], dv[:, :, 0, :], ACT.Exp, scale=-1.0))
                    signal(f"E{n}", act.activation(ev[:, :, 1, :], dv[:, :, 1, :], ACT.Exp))
                act.wait_ge(at_pe, after(AT_PE, c, "O"))
                signal("SQ", act.activation(sq[:, :, :], bank(5).rearrange("s (h n) -> s h n", n=P), ACT.Square))
                dve_done("SS")
                signal("LN", act.activation(rs[:, 2, 0:4], ss[:, 2, 0:4], ACT.Ln, scale=1.0 / P, bias=EPS))
                act.wait_ge(at_act, after(AT_ACT, c, "LN"))
                signal("RSTD", act.activation(rs[:, 2, 4:8], rs[:, 2, 0:4], ACT.Exp, scale=-0.5))
                apart(act, (at_dve, after(AT_DVE, c, "MIX", AT_DVE0)))
                signal("HI", act.activation(hb_hi[:, :, cols], mixf[:, :, :], ACT.Copy))
                assert order == AT_ACT, order

            for t in range(CT):
                act.wait_ge(ln_dve, t + 1)
                if t >= 2:
                    act.wait_ge(ln_pe, 1 + t - 1)
                act.activation(ln_sq[:, t % 2, :], y4[:, t, :], ACT.Square).then_inc(ln_act, 1)
            act.wait_ge(ln_pe, 1 + CT)
            me.done(act.activation(ln_rs[:, :], pair[1][:, :], ACT.Ln, scale=1.0 / (CT * P), bias=EPS))
            me.wait()
            act.activation(ln_rs[:, :], ln_rs[:, :], ACT.Exp, scale=-0.5).then_inc(ln_act, 1)
            for t in range(CT):
                act.wait_ge(ln_dve, CT + t + 1 + max(0, t - 1))
                act.activation(ln_f[:, t % 2, :], y4[:, t, :], ACT.Silu, scale=vec[:, ROW_LNG + t:ROW_LNG + t + 1],
                               bias=vec[:, ROW_LNB + t:ROW_LNB + t + 1]).then_inc(ln_act, 1)
                act.wait_ge(ln_act, CT + 1 + 2 * t + 1)
                act.activation(ha_hi[:, t, :], ln_f[:, t % 2, :], ACT.Copy).then_inc(ln_act, 1)

            def mix_out(n, j, count):
                apart(act, (w_used, count))
                act.activation(mt[:, n, :], pair[j][:, :], ACT.Copy).then_inc(mt_ready, 1)
            act.wait_ge(ln_dve, LN_DVE)
            with act.Fori(0, 4, 3) as n0:
                for j in range(3):
                    mix_out(n0 + j, j, n0 + (N_IN + j + 1))
            for n in (6, 7):
                mix_out(n, n % 3, N_IN + n + 1)

            def tail_norm(call, i):
                act.wait_ge(tail_turned, TT * call + i + 1)
                root_mean_square(pair[i % 2][:, :], pair[2][:, :], i, 1, D).then_inc(tail_ss, 1)

            def x1_norm(i):
                act.wait_ge(tail_done, i + 1)
                root_mean_square(x1[:, i, :], pair[2][:, :], i, 3, D).then_inc(x1_ss, 1)
            act.wait_ge(mt_ready, N_OUT)
            for i in range(TT):
                tail_norm(0, i)
                if i:
                    x1_norm(i - 1)
            x1_norm(TT - 1)
            hi_parts(1, full1)

            F0 = N_IN + N_OUT

            def silu_gate(e, used, first=False):
                act.wait_ge(w_used, used)
                if not first:
                    act.wait_ge(ufull_ready, e)
                act.activation(gate[:, :], pair[0][:, :], ACT.Silu).then_inc(gate_silu, 1)

            def u_hi_part(e, slot):
                act.wait_ge(ufull_ready, e + 1)
                act.activation(u_hi[:, slot, :], ufull[:, :], ACT.Copy).then_inc(uhi_ready, 1)
            act.wait_ge(h_ready, 32)
            silu_gate(0, F0 + 1, first=True)
            u_hi_part(0, 0)
            with act.Fori(0, FB - 1) as bk:
                silu_gate(bk * 2 + 1, bk * 6 + (F0 + 3))
                u_hi_part(bk * 2 + 1, 1)
                silu_gate(bk * 2 + 2, bk * 6 + (F0 + 5))
                act.wait_ge(w_used, bk * 6 + (F0 + 8))
                u_hi_part(bk * 2 + 2, 0)
            silu_gate(FFT - 1, 6 * (FB - 1) + F0 + 3)
            u_hi_part(FFT - 1, 1)
            for i in range(TT):
                tail_norm(1, i)

        @block.vector
        def _(dve):
            me = Tally(dve, dve_self)
            for s_ in (tap_done, ada_used, modt_ready, y_added):
                dve.sem_inc(s_, CREDIT)
            me.done(dve.memset(scan_keep[:, :], 1.0))
            me.wait()
            me.done(dve.memset(scan_keep[:, 0:S:CHUNK], 0.0))
            dve.wait_ge(vec_turned, 1)
            dve.tensor_copy(vec[:, :], pair[3][:, 0:ROWS]).then_inc(vec_ready, 1)
            me.done(dve.tensor_copy(conv_w_col[:, :], pair[3][:, P:P + TAPS * CT]))
            dve.wait_ge(vec_ready, 1)
            lbv = vec[:, ROW_LB:ROW_LB + HEADS]
            dve.tensor_tensor(lb_tmp[:, 0, :], lbv, lbv, ALU.subtract).then_inc(vec_ready, 1)
            dve.wait_ge(cond_ready, 2)
            me.done(dve.reciprocal(lb_tmp[:, 2, :], lb_tmp[:, 1, :]))
            me.wait()
            me.done(dve.tensor_tensor(lb_tmp[:, 3, :], lb_tmp[:, 1, :], lb_tmp[:, 2, :], ALU.mult))
            me.wait()
            me.done(dve.tensor_tensor(lb_tmp[:, 2, :], lb_tmp[:, 3, :], lb_tmp[:, 3, :], ALU.subtract))
            me.wait()
            dve.tensor_scalar(one_less_lb[:, :], lb_tmp[:, 2, :], -1.0, 1.0, ALU.mult, ALU.add).then_inc(vec_ready, 1)

            def normalise(dst, src, col, which):
                me.done(dve.reciprocal(rs[:, which, col:col + 1], rs[:, which, col:col + 1]))
                me.wait()
                return dve.tensor_scalar(dst, src, rs[:, which, col:col + 1], None, ALU.mult)

            for kt in range(KT):
                dve.wait_ge(ada0_loaded[kt % 3], 16 * (kt // 3 + 1))
                if kt == 0:
                    dve.wait_ge(cond_ready, 1)
                    i_ = dve.tensor_scalar(acc0[:, :], ada0[:, 0, :], cond[:, 0:1], None, ALU.mult)
                else:
                    dve.wait_ge(ada0_used, kt)
                    i_ = dve.scalar_tensor_tensor(out=acc0[:, :], in0=ada0[:, kt % 3, :], scalar=cond[:, kt:kt + 1],
                                                  in1=acc0[:, :], op0=ALU.mult, op1=ALU.add)
                i_.then_inc(ada0_used, 1)
                dve.wait_ge(ss_ready, kt + 1)
                normalise(x0[:, kt, :], x0[:, kt, :], kt, 0).then_inc(xs_ready, 1)
            dve.wait_ge(mod0_summed, 1)
            me.done(dve.tensor_tensor(mod[:, 0:16], pair[3][:, 256:272], vec[:, ROW_BADA:ROW_BADA + 16], ALU.add))
            me.wait()
            dve.scalar_tensor_tensor(out=gs[:, 0, :], in0=mod[:, 8:16], scalar=1.0,
                                     in1=vec[:, ROW_GPRE1:ROW_GPRE1 + KT], op0=ALU.add, op1=ALU.mult).then_inc(mod_ready, 1)
            dve.wait_ge(mod_ready, 1)

            def modulate(call, full, shift):
                def lo(g):
                    kt, half = g // 2, g % 2
                    dve.wait_ge(hi_ready, 16 * call + g + 1)
                    cols = slice(half * HALF, (half + 1) * HALF)
                    hi = (ha_hi if kt < 4 else hb_hi)[:, kt % 4, cols]
                    dve.tensor_tensor((ha_lo if kt < 4 else hb_lo)[:, kt % 4, cols], full[:, g % 2, :], hi,
                                      ALU.subtract).then_inc(h_ready, 1)
                for g in range(16):
                    kt = g // 2
                    dve.wait_ge(turned, 16 * call + g + 1)
                    if g >= 2:
                        dve.wait_ge(h_ready, 16 * call + g - 1)
                    dve.tensor_scalar(full[:, g % 2, :], bank(g % 4), gs[:, call, kt:kt + 1],
                                      mod[:, shift + kt:shift + kt + 1], ALU.mult, ALU.add).then_inc(full_ready, 1)
                    if g:
                        lo(g - 1)
                lo(15)
            modulate(0, full0, 0)

            dve.wait_ge(h_ready, 16)
            me.done(dve.memset(u[:, 0:TAPS - 1], 0.0))
            IN_DVE = 4 + 3
            cwv = conv_w_col[:, :].rearrange("p (j t) -> p j t", t=CT)
            with dve.Fori(0, 4) as t:
                me.enter(t, IN_DVE)
                dve.wait_ge(tap_done, t * 2 * TAPS + CREDIT)
                me.wait()
                me.done(dve.tensor_copy(tile_w[:, :], cwv[:, :, t]))
                me.done(dve.tensor_copy(tile_cols[:, 0:1], vec[:, ds(t + ROW_CB, 1)]))
                me.done(dve.tensor_copy(tile_cols[:, 1:2], one_less_lb[:, ds(t, 1)]))
                me.done(dve.tensor_copy(lb_tmp[:, 0, 0:1], log_one_less_lb[:, ds(t, 1)]))
                for j in range(KT):
                    dve.wait_ge(ada_loaded[j % 2], t * 16 * (KT // 2) + 16 * (j // 2 + 1))
                    if j == 0:
                        i_ = dve.tensor_scalar(acc[:, :], ada[:, 0, :], cond[:, 0:1], None, ALU.mult)
                    else:
                        dve.wait_ge(ada_used, t * KT + j + CREDIT)
                        i_ = dve.scalar_tensor_tensor(out=acc[:, :], in0=ada[:, j % 2, :], scalar=cond[:, j:j + 1],
                                                      in1=acc[:, :], op0=ALU.mult, op1=ALU.add)
                    i_.then_inc(ada_used, 1)
                me.wait()
                dve.wait_ge(gate_sig, t + 1)
                dve.wait_ge(w_used, t * 6 + 2)
                dve.tensor_tensor(u[:, TAPS - 1:], u[:, TAPS - 1:], pair[1][:, :], ALU.mult).then_inc(u_evac, 1)
                dve.wait_ge(u_evac, t + 1)
                dve.wait_ge(y_stored, t * 16 + 16 * CREDIT)

                def taps(lo, hi):
                    for j in range(lo, hi):
                        for h in range(2):
                            dst = y[:, h * HALF:(h + 1) * HALF]
                            src = u[:, h * HALF + j:h * HALF + j + HALF]
                            if j == 0:
                                i_ = dve.tensor_scalar(dst, src, tile_w[:, 0:1], tile_cols[:, 0:1], ALU.mult, ALU.add)
                            else:
                                dve.wait_ge(tap_done, t * 2 * TAPS + (2 * j + h - 1) + CREDIT)
                                i_ = dve.scalar_tensor_tensor(out=dst, in0=src, scalar=tile_w[:, j:j + 1], in1=dst,
                                                              op0=ALU.mult, op1=ALU.add)
                            i_.then_inc(tap_done, 1)
                taps(0, 11)
                dve.wait_ge(z_log, t + 1)
                dve.scalar_tensor_tensor(out=b[:, t, :], in0=pair[0][:, :], scalar=0.0, in1=b[:, t, :],
                                         op0=ALU.min, op1=ALU.subtract).then_inc(z_evac, 1)
                dve.wait_ge(z_evac, t + 1)
                me.done(dve.tensor_scalar(b[:, t, :], b[:, t, :], lb_tmp[:, 0, 0:1], None, ALU.add))
                me.done(dve.tensor_scalar(k[:, t, :], k[:, t, :], tile_cols[:, 1:2], None, ALU.mult))
                me.wait()
                me.done(dve.tensor_tensor_scan(b[:, t, :], scan_keep[:, :], b[:, t, :], 0.0, ALU.mult, ALU.add))
                taps(11, TAPS)
                dve.wait_ge(modt_summed, t + 1)
                dve.tensor_tensor(mod[:, ds(t * KT + 16, KT)], pair[3][:, 288:288 + KT],
                                  vec[:, ds(t * KT + (ROW_BADA + 16), KT)], ALU.add).then_inc(modt_ready, 1)
            me.leave(4)
            dve.wait_ge(modt_ready, 4 + CREDIT)
            dve.scalar_tensor_tensor(out=gs[:, 1, :], in0=mod[:, 32:40], scalar=1.0,
                                     in1=vec[:, ROW_GPRE2:ROW_GPRE2 + KT], op0=ALU.add, op1=ALU.mult).then_inc(mod_ready, 1)
            dve.tensor_tensor(gg[:, 0, :], mod[:, 16:24], vec[:, ROW_GPOST1:ROW_GPOST1 + KT], ALU.mult).then_inc(mod_ready, 1)
            dve.tensor_tensor(gg[:, 1, :], mod[:, 40:48], vec[:, ROW_GPOST2:ROW_GPOST2 + KT], ALU.mult).then_inc(mod_ready, 1)

            me.wait()
            dve.wait_ge(w_used, N_IN)
            dve.wait_ge(v_ready, HEADS + CREDIT)
            dve.wait_ge(og_stored, 16 * HEADS + 16 * CREDIT)
            dve.wait_ge(y_stored, 16 * CT + 16 * CREDIT)
            dve.wait_ge(v_turned, 4)
            dve.wait_ge(consts_ready, 3)
            dve.memset(pmat[:, :, :], 0.0).then_inc(at_dve, 1)
            dve.memset(state[:, :, :, :], 0.0).then_inc(at_dve, 1)
            dve.wait_ge(at_dve, 2)
            with dve.Fori(0, TT // 2) as half_c:
                for par in range(2):
                    c = half_c * 2 + par
                    order = []

                    def emit(name, i_):
                        i_.then_inc(at_dve, 1)
                        order.append(name)

                    def own(name):
                        dve.wait_ge(at_dve, after(AT_DVE, c, name, AT_DVE0))

                    def act_done(name):
                        dve.wait_ge(at_act, after(AT_ACT, c, name))

                    def pe_done(name):
                        dve.wait_ge(at_pe, after(AT_PE, c, name))
                    cols = ds(c * P, P)
                    bch = b[:, :, cols].rearrange("p h (g c) -> p h g c", c=CHUNK)
                    emit("DKD", dve.tensor_tensor(dd[:, 1].rearrange("p h (g c) -> p h g c", c=CHUNK), bch,
                                                  bch[:, :, :, CHUNK - 1:CHUNK].to_broadcast([P, HEADS, 2, CHUNK]), ALU.subtract))

                    def diff(n):
                        size = LEVELS[n]
                        bv = b[:, :, cols].rearrange("p h (g c) -> p h g c", c=size)
                        ref = bv[:, :, :, size // 2 - 1:size // 2].to_broadcast([P, HEADS, P // size, size])
                        emit(f"D{n}", dve.tensor_tensor(dd[:, n % 2].rearrange("p h (g c) -> p h g c", c=size), bv, ref, ALU.subtract))

                    def scaled(n):
                        size = LEVELS[n]
                        act_done(f"E{n}")
                        ev, xv, kv, qv = (w.rearrange("p h (g s c) -> p h g s c", s=2, c=size // 2)
                                          for w in (ee[:, n % 2], xr[:, n % 3], k[:, :, cols], q[:, :, cols]))
                        emit(f"XL{n}", dve.tensor_tensor(xv[:, :, :, 0, :], kv[:, :, :, 0, :], ev[:, :, :, 0, :], ALU.mult))
                        emit(f"X{n}", dve.tensor_tensor(xv[:, :, :, 1, :], qv[:, :, :, 1, :], ev[:, :, :, 1, :], ALU.mult))

                    def place(name, mask, src):
                        emit(name, dve.copy_predicated(pmat[:, :, :],
                                                       mask.bitcast(I32).unsqueeze(1).to_broadcast([P, HEADS, P]),
                                                       src.rearrange("s (h n) -> s h n", n=P)))

                    def level_in(n):
                        apart(dve, (at_pe, after(AT_PE, c, f"S{n}")), (at_dve, after(AT_DVE, c, f"P{n - 1}" if n else "PD", AT_DVE0)))
                        place(f"P{n}", masks[:, n, :], bank((n + 1) % 2))
                    diff(0)
                    act_done("EKD")
                    emit("KD", dve.tensor_tensor(kd[:, :, :], k[:, :, cols], ee[:, 1], ALU.mult))
                    act_done("EB")
                    emit("QE", dve.tensor_tensor(qe[:, :, :], q[:, :, cols], eb[:, :, :], ALU.mult))
                    diff(1)
                    scaled(0)
                    diff(2)
                    scaled(1)
                    apart(dve, (at_pe, after(AT_PE, c, "DIAG")))
                    place("PD", ident[:, :], bank(0))
                    level_in(0)
                    diff(3)
                    scaled(2)
                    level_in(1)
                    diff(4)
                    scaled(3)
                    level_in(2)
                    diff(5)
                    scaled(4)
                    level_in(3)
                    scaled(5)
                    level_in(4)
                    pe_done("C0")
                    for h in range(HEADS):
                        emit("ST1", dve.scalar_tensor_tensor(out=state[:, 1, h, :], in0=state[:, 0, h, :],
                                                             scalar=eb[:, h, CHUNK - 1:CHUNK], in1=bank(3)[:, h * P:(h + 1) * P],
                                                             op0=ALU.mult, op1=ALU.add))
                    level_in(5)
                    act_done("SQ")
                    emit("SS", dve.tensor_reduce(ss[:, 2, 0:4], sq[:, :, :], AX_X, ALU.add))
                    pe_done("O")
                    own("ST1")
                    for h in range(HEADS):
                        emit("ST0", dve.scalar_tensor_tensor(out=state[:, 0, h, :], in0=state[:, 1, h, :],
                                                             scalar=eb[:, h, P - 1:P], in1=bank(4)[:, h * P:(h + 1) * P],
                                                             op0=ALU.mult, op1=ALU.add))
                    act_done("RSTD")
                    emit("ON", dve.tensor_tensor(on[:, :, :], bank(5).rearrange("s (h n) -> s h n", n=P),
                                                 rs[:, 2, 4:8].unsqueeze(2).to_broadcast([P, HEADS, P]), ALU.mult))
                    pe_done("OT")
                    dve.wait_ge(ogc_loaded[par], half_c * 16 + 16)
                    emit("MIX", dve.scalar_tensor_tensor(out=mixf[:, :, :], in0=bank(6).rearrange("p (h n) -> p h n", n=P),
                                                         scalar=vec[:, ROW_NG:ROW_NG + 1], in1=ogc[:, par], op0=ALU.mult, op1=ALU.mult))
                    act_done("HI")
                    emit("LO", dve.tensor_tensor(hb_lo[:, :, cols], mixf[:, :, :], hb_hi[:, :, cols], ALU.subtract))
                    assert order == AT_DVE, order

            dve.wait_ge(ln_pe, 1)
            for t in range(CT):
                dve.scalar_tensor_tensor(out=y4[:, t, :], in0=pair[0][:, :], scalar=-1.0 / (CT * P), in1=y4[:, t, :],
                                         op0=ALU.mult, op1=ALU.add).then_inc(ln_dve, 1)
            dve.wait_ge(ln_act, CT + 1)

            def ln_lo(t):
                dve.wait_ge(ln_act, CT + 1 + 2 * (t + 1))
                dve.tensor_tensor(ha_lo[:, t, :], ln_f[:, t % 2, :], ha_hi[:, t, :], ALU.subtract).then_inc(ln_dve, 1)
            for t in range(CT):
                dve.tensor_tensor(y4[:, t, :], y4[:, t, :], ln_rs[:, :], ALU.mult).then_inc(ln_dve, 1)
                if t:
                    ln_lo(t - 1)
            ln_lo(CT - 1)

            def residual(call, i, tmp):
                dve.wait_ge(tail_ss, TT * call + i + 1)
                me.done(dve.reciprocal(rs[:, 1, i:i + 1], rs[:, 1, i:i + 1]))
                me.wait()
                me.done(dve.scalar_tensor_tensor(out=tmp, in0=pair[i % 2][:, :], scalar=rs[:, 1, i:i + 1], in1=ggb[:, :],
                                                 op0=ALU.mult, op1=ALU.mult))
                me.wait()
                dve.tensor_tensor(x1[:, i, :], x1[:, i, :], tmp, ALU.add).then_inc(tail_done, 1)

            def gg_rows(call):
                dve.wait_ge(ggb_pe, call + 1)
                dve.tensor_copy(ggb[:, :], pair[3][:, :]).then_inc(ggb_ready, 1)
                dve.wait_ge(ggb_ready, call + 1)
            gg_rows(0)
            dve.wait_ge(x1_loaded, 16)
            for i in range(TT):
                residual(0, i, xs[:, i, :])
                if i:
                    dve.wait_ge(x1_ss, i)
                    normalise(xs[:, i - 1, :], x1[:, i - 1, :], i - 1, 3).then_inc(xs_ready, 1)
            dve.wait_ge(x1_ss, TT)
            normalise(xs[:, TT - 1, :], x1[:, TT - 1, :], TT - 1, 3).then_inc(xs_ready, 1)
            dve.wait_ge(tail_turned, TT)
            modulate(1, full1, 24)

            dve.wait_ge(h_ready, 32)
            dve.memset(mt[:, :, :], 0.0).then_inc(yt_zero, 1)
            dve.wait_ge(yt_zero, 1)

            def u_full(e, used, first=False):
                dve.wait_ge(gate_silu, e + 1)
                dve.wait_ge(w_used, used)
                if not first:
                    dve.wait_ge(u_ready, e)
                dve.tensor_tensor(ufull[:, :], gate[:, :], pair[1][:, :], ALU.mult).then_inc(ufull_ready, 1)

            def u_low(e, slot):
                dve.wait_ge(uhi_ready, e + 1)
                dve.tensor_tensor(u_lo[:, slot, :], ufull[:, :], u_hi[:, slot, :], ALU.subtract).then_inc(u_ready, 1)

            def add_down(bk, used):
                for n in range(KT):
                    if n < KT - 1:
                        dve.wait_ge(down_ready, bk * (KT - 1) + (n + 1))
                    else:
                        dve.wait_ge(w_used, used)
                    dve.tensor_tensor(mt[:, n, :], mt[:, n, :], pair[2 + n % 2][:, :], ALU.add).then_inc(y_added, 1)
            F0 = N_IN + N_OUT
            u_full(0, F0 + 2, first=True)
            u_low(0, 0)
            with dve.Fori(0, FB - 1) as bk:
                u_full(bk * 2 + 1, bk * 6 + (F0 + 4))
                u_low(bk * 2 + 1, 1)
                u_full(bk * 2 + 2, bk * 6 + (F0 + 6))
                add_down(bk, bk * 6 + (F0 + 8))
                u_low(bk * 2 + 2, 0)
            u_full(FFT - 1, 6 * (FB - 1) + F0 + 4)
            u_low(FFT - 1, 1)
            add_down(FB - 1, 6 * (FB - 1) + F0 + 6)
            gg_rows(1)
            for i in range(TT):
                residual(1, i, tail_tmp[:, i % 2, :])

        @block.tensor
        def _(pe):
            pe.wait_ge(consts_ready, 2)
            pe.wait_ge(vec_loaded, 16 * VEC_LOADS)
            pe.transpose(pair[3][:, 0:ROWS], rows_a[:, :], ident[0:ROWS, 0:ROWS])
            pe.transpose(pair[3][:, P:P + TAPS * CT], rows_b[:, :], ident[0:TAPS * CT, 0:TAPS * CT]).then_inc(vec_turned, 1)

            def column_sums(src, dst, tiles):
                for n in range(tiles):
                    i_ = pe.matmul(dst[:, n:n + 1], src[:, n * P:(n + 1) * P], ones[:, 0:1], start=True, stop=True)
                return i_
            pe.wait_ge(ada0_used, KT)
            pe.wait_ge(vec_ready, 2)
            column_sums(acc0, pair[3][:, 256:272], 16).then_inc(mod0_summed, 1)

            def turn_tiles(call, src):
                for g in range(16):
                    kt, half = g // 2, g % 2
                    if g >= 4:
                        pe.wait_ge(full_ready, 16 * call + g - 3)
                    for i in range(4):
                        tile = 4 * half + i
                        pe.wait_ge(xs_ready, TT * call + tile + 1)
                        i_ = pe.transpose(bank(g % 4)[:, i * P:(i + 1) * P], src[:, tile, kt * P:(kt + 1) * P], ident[:, :])
                    i_.then_inc(turned, 1)
            turn_tiles(0, x0)

            def split_product(dst, slot, w_cols, x_hi, x_lo, first, last):
                wh, wl = w_hi[:, slot, w_cols], w_lo[:, slot, w_cols]
                steps = [(wh, x_hi), (wh, x_lo), (wl, x_hi)]
                for s_, (w, x) in enumerate(steps):
                    for half in range(2):
                        cols = slice(half * HALF, (half + 1) * HALF)
                        i_ = pe.matmul(dst[:, cols], w, x[:, cols], start=first and s_ == 0, stop=last and s_ == 2)
                return i_

            def project(dst, slot):
                for kt in range(KT):
                    hi, lo = (ha_hi, ha_lo) if kt < 4 else (hb_hi, hb_lo)
                    i_ = split_product(dst, slot, slice(kt * P, (kt + 1) * P), hi[:, kt % 4, :], lo[:, kt % 4, :],
                                       kt == 0, kt == KT - 1)
                return i_

            pe.wait_ge(h_ready, 16)
            with pe.Fori(0, 4) as t:
                free = [(og_evac, t + CREDIT), (vt_evac, t + CREDIT), (gate_sig, t + 1), (u_evac, t + 1), (z_evac, t + 1), (q_evac, t + 1)]
                for j in range(6):
                    pe.wait_ge(w_split, t * 6 + (j + 1))
                    pe.wait_ge(*free[j])
                    project(pair[j % 2], j % WS).then_inc(w_used, 1)
                    if j == 2:
                        pe.wait_ge(ada_used, t * KT + KT + CREDIT)
                        pe.wait_ge(modt_ready, t + CREDIT)
                        column_sums(acc, pair[3][:, 288:288 + KT], KT).then_inc(modt_summed, 1)
                pe.wait_ge(vt_evac, t + 1 + CREDIT)
                pe.wait_ge(v_ready, t + CREDIT)
                for c in range(TT):
                    i_ = pe.transpose(pair[2][:, c * P:(c + 1) * P], vt[:, c * P:(c + 1) * P], ident[:, :])
                i_.then_inc(v_turned, 1)

            pe.wait_ge(modt_ready, 4 + CREDIT)
            pe.wait_ge(v_ready, 4 + CREDIT)
            with pe.Fori(0, TT) as c:
                order = []

                def signal(name, i_):
                    i_.then_inc(at_pe, 1)
                    order.append(name)

                def dve_done(name):
                    pe.wait_ge(at_dve, after(AT_DVE, c, name, AT_DVE0))
                dve_done("KD")
                for h in range(HEADS):
                    i_ = pe.transpose(bank(2)[:, h * P:(h + 1) * P], kd[:, h, :], ident[:, :])
                signal("KDT", i_)
                pe.wait_ge(at_act, after(AT_ACT, c, "KC"))
                for h in range(HEADS):
                    i_ = pe.matmul(bank(0)[:, h * P:(h + 1) * P], kc[:, h, :], q[:, h, ds(c * P, P)], start=True, stop=True)
                signal("DIAG", i_)
                for n in range(len(LEVELS)):
                    dve_done(f"X{n}")
                    if n:
                        dve_done("PD" if n == 1 else f"P{n - 2}")
                    for h in range(HEADS):
                        i_ = pe.matmul(bank((n + 1) % 2)[:, h * P:(h + 1) * P], xr[:, n % 3, h, :], xr[:, n % 3, h, :],
                                       start=True, stop=True)
                    signal(f"S{n}", i_)
                pe.wait_ge(at_act, after(AT_ACT, c, "KDT"))
                for j in range(2):
                    rows = slice(j * CHUNK, (j + 1) * CHUNK)
                    for h in range(HEADS):
                        i_ = pe.matmul(bank(3 + j)[:, h * P:(h + 1) * P], kdt[rows, h, :], vc[rows, h, :], start=True, stop=True)
                    signal(f"C{j}", i_)
                dve_done("P5")
                for h in range(HEADS):
                    o = bank(5)[:, h * P:(h + 1) * P]
                    pe.matmul(o, pmat[:, h, :], vc[:, h, :], start=True, stop=False, skip_group_check=True)
                    for j in range(2):
                        rows = slice(j * CHUNK, (j + 1) * CHUNK)
                        i_ = pe.matmul(o[rows, :], qe[:, h, rows], state[:, j, h, :], start=False, stop=True, skip_group_check=True)
                signal("O", i_)
                dve_done("ON")
                for h in range(HEADS):
                    i_ = pe.transpose(bank(6)[:, h * P:(h + 1) * P], on[:, h, :], ident[:, :])
                signal("OT", i_)
                assert order == AT_PE, order

            pe.wait_ge(y4_loaded, 16)
            for t in range(CT):
                for half in range(2):
                    cols = slice(half * HALF, (half + 1) * HALF)
                    i_ = pe.matmul(pair[0][:, cols], ones[:, :], y4[:, t, cols], start=t == 0, stop=t == CT - 1)
            i_.then_inc(ln_pe, 1)
            for t in range(CT):
                pe.wait_ge(ln_act, t + 1)
                for half in range(2):
                    cols = slice(half * HALF, (half + 1) * HALF)
                    i_ = pe.matmul(pair[1][:, cols], ones[:, :], ln_sq[:, t % 2, cols], start=t == 0, stop=t == CT - 1)
                i_.then_inc(ln_pe, 1)

            def gg_rows(call):
                for n in range(KT):
                    i_ = pe.matmul(pair[3][:, n * P:(n + 1) * P], gg[:, call, n:n + 1].to_broadcast([P, P]), ident[:, :],
                                   start=True, stop=True)
                i_.then_inc(ggb_pe, 1)
            pe.wait_ge(mod_ready, 4)
            pe.wait_ge(at_dve, after(AT_DVE, TT - 1, "LO", AT_DVE0))
            gg_rows(0)

            pe.wait_ge(ln_dve, LN_DVE)

            def out_tile(j, need, free, slot):
                pe.wait_ge(w_split, need)
                if free is not None:
                    pe.wait_ge(mt_ready, free)
                project(pair[j], slot).then_inc(w_used, 1)
            pe.wait_ge(ggb_ready, 1)
            for j in range(3):
                out_tile(j, N_IN + j + 1, None, (N_IN + j) % WS)
            for n in range(3, N_OUT):
                out_tile(n % 3, N_IN + n + 1, n - 2, (N_IN + n) % WS)

            def turn_back(call, src):
                for i in range(TT):
                    if i >= 2:
                        pe.wait_ge(tail_done, TT * call + i - 1)
                    for n in range(KT):
                        i_ = pe.transpose(pair[i % 2][:, n * P:(n + 1) * P], src[:, n, i * P:(i + 1) * P], ident[:, :])
                    i_.then_inc(tail_turned, 1)
            pe.wait_ge(mt_ready, N_OUT)
            turn_back(0, mt)
            pe.wait_ge(tail_done, TT)
            turn_tiles(1, xs)

            pe.wait_ge(h_ready, 32)
            F0 = N_IN + N_OUT

            def gate_up(e, need, slot, first=False):
                pe.wait_ge(w_split, need + 1)
                if not first:
                    pe.wait_ge(gate_silu, e)
                project(pair[0], slot % WS).then_inc(w_used, 1)
                pe.wait_ge(w_split, need + 2)
                if not first:
                    pe.wait_ge(ufull_ready, e)
                project(pair[1], (slot + 1) % WS).then_inc(w_used, 1)

            def down(bk, need, slot):
                pe.wait_ge(w_split, need + 2)
                pe.wait_ge(u_ready, bk * 2 + 2)
                for n in range(KT):
                    if n < 2:
                        pe.wait_ge(y_added, bk * KT + CREDIT)
                    else:
                        pe.wait_ge(y_added, bk * KT + (n - 1) + CREDIT)
                    for f in range(2):
                        i_ = split_product(pair[2 + n % 2], (slot + f) % WS, slice(n * P, (n + 1) * P), u_hi[:, f, :],
                                           u_lo[:, f, :], f == 0, f == 1)
                    if n < KT - 1:
                        i_.then_inc(down_ready, 1)
                    else:
                        i_.then_inc(w_used, 2)
            gate_up(0, F0, F0, first=True)
            with pe.Fori(0, FB - 1) as bk:
                gate_up(bk * 2 + 1, bk * 6 + (F0 + 2), F0 + 2)
                gate_up(bk * 2 + 2, bk * 6 + (F0 + 4), F0 + 4)
                down(bk, bk * 6 + (F0 + 6), F0 + 6)
            gate_up(FFT - 1, 6 * (FB - 1) + F0 + 2, F0 + 2)
            down(FB - 1, 6 * (FB - 1) + F0 + 4, F0 + 4)
            pe.wait_ge(y_added, FB * KT + CREDIT)
            gg_rows(1)
            turn_back(1, mt)


_SHAPES = [("x", (1, S, D)), ("c", (1, D)), ("w_ada", (1, D, 6 * D)), ("b_ada", (1, 6 * D)), ("g_pre_mix", (1, D)),
           ("g_post_mix", (1, D)), ("w_in", (1, D, 3 * D)), ("conv_w", (1, TAPS, CT * P)), ("conv_b", (1, CT * P)),
           ("conv_ln_g", (1, CT * P)), ("conv_ln_b", (1, CT * P)), ("hgrn_lower_bounds", (1, HEADS * P)),
           ("hgrn_norm_g", (1, P)), ("w_out", (1, D, D)), ("g_pre_ffn", (1, D)), ("g_post_ffn", (1, D)),
           ("w_ffn_in", (1, D, 2 * D_FF)), ("w_ffn_out", (1, D_FF, D))]


def kernel(**inputs):
    import numpy as np
    import concourse.bacc as bacc
    from concourse.bass_utils import run_bass_kernel_spmd

    nc = bacc.Bacc("TRN2", target_bir_lowering=False, num_devices=1)
    arrays, t_in = {}, {}
    for name, shape in _SHAPES:
        a = np.ascontiguousarray(inputs[name])
        assert a.shape == shape, (name, a.shape)
        arrays[f"in_{name}"] = a
        t_in[name] = nc.dram_tensor(f"in_{name}", a.shape, mybir.dt.from_np(a.dtype), kind="ExternalInput").ap()
    out = nc.dram_tensor("out", (1, S, D), F32, kind="ExternalOutput").ap()
    build(nc, t_in, out)
    result = run_bass_kernel_spmd(nc, [arrays], core_ids=[0])
    return result.results[0]["out"]
```

```python
from contextlib import ExitStack

import concourse.bass as bass
from concourse import mybir

F32 = mybir.dt.float32
F32R = mybir.dt.float32r
BF16 = mybir.dt.bfloat16
I32 = mybir.dt.int32
ALU = mybir.AluOpType
ACT = mybir.ActivationFunctionType
AX_X = mybir.AxisListType.X
ds = bass.ds

P = 128
D = 1024
S = 1024
KT = D // P
TT = S // P
HALF = 512
CHUNK = 64
TAPS = 31
HEADS = 4
CT = 4
FFT = 22
FB = FFT // 2
D_FF = FFT * P
EPS = 1e-6
LEVELS = [64, 32, 16, 8, 4, 2]

RAW = 2
WS = 3
N_IN = 6 * 4
N_OUT = KT
N_FFN = 3 * FFT
N_CHUNKS = N_IN + N_OUT + N_FFN

ROW_C, ROW_GPRE1, ROW_GPOST1, ROW_GPRE2, ROW_GPOST2 = 0, 8, 16, 24, 32
ROW_BADA, ROW_CB, ROW_LNG, ROW_LNB, ROW_LB, ROW_NG, ROWS = 40, 88, 92, 96, 100, 104, 105


POOL_F = ["DKD", "D0", "KD", "QE", "D1", "D2", "D3", "D4", "D5"]
POOL_B = ["LO"]
ACT_F = ["KC", "VC", "EKD", "EB", "EL0", "E0", "EL1", "E1", "KDT", "EL2", "E2", "EL3", "E3", "EL4", "E4", "EL5", "E5"]
ACT_B = ["SQ", "LN", "RSTD", "HI"]
DVE_F = ["XL0", "X0", "XL1", "X1", "PD", "P0", "XL2", "X2", "P1", "XL3", "X3", "P2", "XL4", "X4", "P3",
         "XL5", "X5", "P4"] + ["ST1"] * 4 + ["ST0"] * 4 + ["P5"]
DVE_B = ["SS", "ON", "MIX"]
PE_F = ["KDT", "DIAG", "S0", "S1", "S2", "C0", "C1", "S3", "S4", "S5"]
PE_B = ["O", "OT"]
VEC_LOADS = 12
CREDIT = 1
LN_DVE = 3 * CT


class Tally:

    def __init__(self, eng, sem):
        self.eng, self.sem, self.base, self.turn, self.per, self.n = eng, sem, 0, 0, 0, 0

    def done(self, instruction):
        instruction.then_inc(self.sem, 1)
        self.n += 1

    def wait(self, behind=0):
        self.eng.wait_ge(self.sem, self.base + self.turn * self.per + self.n - behind)

    def last(self):
        return self.sem, self.base + self.turn * self.per + self.n

    def enter(self, turn, per):
        self.base, self.turn, self.per, self.n = self.base + self.n, turn, per, 0

    def leave(self, turns):
        assert self.n == self.per, (self.n, self.per)
        self.base, self.turn, self.per, self.n = self.base + self.per * turns, 0, 0, 0


def build(nc, t_in, out):
    x_d = t_in["x"].rearrange("a (i p) d -> (a p) i d", p=P)
    out_d = out.rearrange("a (i p) d -> (a p) i d", p=P)
    w_ada_d = t_in["w_ada"].rearrange("l (kt p) n -> (l p) kt n", p=P)
    w_in_d = t_in["w_in"].rearrange("l (kt p) n -> (l p) kt n", p=P)
    w_out_d = t_in["w_out"].rearrange("l (kt p) n -> (l p) kt n", p=P)
    w_up_d = t_in["w_ffn_in"].rearrange("l (kt p) n -> (l p) kt n", p=P)
    w_down_d = t_in["w_ffn_out"].rearrange("l (f p) n -> (l p) f n", p=P)
    y_spill = nc.dram_tensor("conv_spill", [P, CT, S], F32).ap()
    og_spill = nc.dram_tensor("og_spill", [P, HEADS, S], F32).ap()

    ctx = ExitStack()
    with ctx:
        def sem(name):
            return ctx.enter_context(nc.semaphore(name))

        def group(specs):
            made = []
            with ExitStack() as place:
                for name, shape, dt in specs:
                    made.append(place.enter_context(nc.sbuf_tensor(name, shape, dt)))
            return made

        def keep(name, shape, dt=F32):
            return ctx.enter_context(nc.sbuf_tensor(name, shape, dt))

        ident = keep("ident", [P, P])
        ones = keep("ones", [P, P])
        masks = keep("masks", [P, len(LEVELS), P])
        scan_keep = keep("scan_keep", [P, S], BF16)
        rows_a = keep("rows_a", [ROWS, P])
        rows_b = keep("rows_b", [TAPS * CT, P])
        vec = keep("vec", [P, ROWS])
        conv_w_col = keep("conv_w_col", [P, TAPS * CT])
        mod = keep("mod", [P, 48])
        cond = keep("cond", [P, KT])
        gs = keep("gs", [P, 2, KT])
        gg = keep("gg", [P, 2, KT])
        lb_tmp = keep("lb_tmp", [P, 5, HEADS])
        one_less_lb = keep("one_less_lb", [P, HEADS])
        log_one_less_lb = keep("log_one_less_lb", [P, HEADS])
        tile_w = keep("tile_w", [P, TAPS])
        tile_cols = keep("tile_cols", [P, 3])
        ss = keep("ss", [P, 4, TT])
        rs = keep("rs", [P, 4, TT])
        ggb = keep("ggb", [P, D])
        raw = keep("raw", [P, RAW, D])
        w_hi = keep("w_hi", [P, WS, D], F32R)
        w_lo = keep("w_lo", [P, WS, D], F32R)

        w2k = [P, HEADS, P]
        xr, dd, ee, qe, kd, kc, kdt, vc = group([
            ("xr", [P, 3, HEADS, P], F32), ("dd", [P, 3, HEADS, P], F32), ("ee", [P, 3, HEADS, P], F32),
            ("qe", [P, 2, HEADS, P], F32), ("kd", w2k, F32), ("kc", w2k, F32), ("kdt", w2k, F32),
            ("vc", [P, 2, HEADS, P], F32)])
        ha_hi = keep("ha_hi", [P, 4, S], F32R)
        ha_lo = keep("ha_lo", [P, 4, S], F32R)
        hb_hi = keep("hb_hi", [P, 4, S], F32R)
        hb_lo = keep("hb_lo", [P, 4, S], F32R)

        x0, ada0, acc0, _, full0 = group([("x0", [P, TT, D], F32), ("ada0", [P, 3, 2 * D], F32),
                                          ("acc0", [P, 2 * D], F32), ("pad0", [P, 16], F32),
                                          ("full0", [P, 2, HALF], F32)])
        q, k, b, v, ada, acc, ogt, vt, sg, u, y = group([
            ("q", [P, HEADS, S], F32), ("k", [P, HEADS, S], F32), ("b", [P, HEADS, S], F32),
            ("v", [P, TT, HEADS * P], F32), ("ada", [P, 2, D], F32), ("acc", [P, D], F32),
            ("ogt", [P, S], F32), ("vt", [P, S], F32), ("sg", [P, S], F32),
            ("u", [P, S + TAPS - 1], F32), ("y", [P, S], F32)])
        _, pmat, state, ogc, mixf, eb, sq, on = group([
            ("qkbv", [P, 4 * HEADS * S], F32), ("pmat", [P, 2, HEADS, P], F32), ("state", [P, 4, HEADS, P], F32),
            ("ogc", [P, 2, HEADS, P], F32), ("mixf", w2k, F32), ("eb", w2k, F32), ("sq", w2k, F32), ("on", w2k, F32)])
        wo_hi, wo_lo, x1, xs, tail_tmp = group([
            ("wo_hi", [P, N_OUT - WS, D], F32R), ("wo_lo", [P, N_OUT - WS, D], F32R), ("x1", [P, TT, D], F32),
            ("xs", [P, 4, D], F32), ("tail_tmp", [P, 2, D], F32)])
        _, y4, ln_sq, ln_rs, ln_f = group([
            ("wo_", [P, 2 * (N_OUT - WS), D], F32), ("y4", [P, CT, S], F32), ("ln_sq", [P, 2, S], F32),
            ("ln_rs", [P, S], F32), ("ln_f", [P, 2, S], F32)])
        _, full1 = group([("before_full1", [P, 2 * (N_OUT - WS) + TT + 4, D], F32), ("full1", [P, 2, HALF], F32)])
        yt, gate, ufull, _, u_hi, u_lo = group([
            ("yt", [P, TT, D], F32), ("gate", [P, S], F32), ("ufull", [P, S], F32), ("x1_", [P, TT, D], F32),
            ("u_hi", [P, 2, S], F32R), ("u_lo", [P, 2, S], F32R)])
        pair = [ctx.enter_context(nc.psum_tensor(f"pair{i}", [P, S], F32)) for i in range(4)]

        def bank(i):
            return pair[i // 2][:, (i % 2) * HALF:(i % 2 + 1) * HALF]

        consts_ready = sem("consts_ready")
        vec_loaded = sem("vec_loaded")
        vec_turned = sem("vec_turned")
        vec_ready = sem("vec_ready")
        cond_ready = sem("cond_ready")
        x_loaded = [sem(f"x_loaded{i}") for i in range(2)]
        x1_loaded = sem("x1_loaded")
        ada0_loaded = [sem(f"ada0_loaded{i}") for i in range(3)]
        ada0_used = sem("ada0_used")
        acc0_ready = sem("acc0_ready")
        mod0_summed = sem("mod0_summed")
        mod_ready = sem("mod_ready")
        ss_ready = sem("ss_ready")
        xs_ready = sem("xs_ready")
        turned = sem("turned")
        full_ready = sem("full_ready")
        hi_ready = sem("hi_ready")
        h_ready = sem("h_ready")
        raw_loaded = [sem(f"raw_loaded{i}") for i in range(RAW)]
        w_split = sem("w_split")
        w_used = sem("w_used")
        gate_sig = sem("gate_sig")
        q_evac = sem("q_evac")
        og_evac = sem("og_evac")
        vt_evac = sem("vt_evac")
        z_evac = sem("z_evac")
        u_evac = sem("u_evac")
        ada_loaded = [sem(f"ada_loaded{i}") for i in range(2)]
        ada_used = sem("ada_used")
        modt_summed = sem("modt_summed")
        modt_ready = sem("modt_ready")
        z_log = sem("z_log")
        tap_done = sem("tap_done")
        y_stored = sem("y_stored")
        og_stored = sem("og_stored")
        v_turned = sem("v_turned")
        v_ready = sem("v_ready")
        act_self = sem("act_self")
        dve_self = sem("dve_self")
        pool_self = sem("pool_self")
        at_pool_f, at_pool_b = sem("at_pool_f"), sem("at_pool_b")
        at_act_f, at_act_b = sem("at_act_f"), sem("at_act_b")
        at_dve_f, at_dve_b = sem("at_dve_f"), sem("at_dve_b")
        at_pe_f, at_pe_b = sem("at_pe_f"), sem("at_pe_b")
        at_clear = sem("at_clear")
        b_ready = sem("b_ready")
        ogc_loaded = [sem(f"ogc_loaded{i}") for i in range(2)]
        y4_loaded = sem("y4_loaded")
        ln_pe = sem("ln_pe")
        ln_dve = sem("ln_dve")
        ln_act = sem("ln_act")
        ggb_pe = sem("ggb_pe")
        ggb_ready = sem("ggb_ready")
        tail_ss = sem("tail_ss")
        tail_read = sem("tail_read")
        tail_done = sem("tail_done")
        last_done = sem("last_done")
        x1_ss = sem("x1_ss")
        gate_silu = sem("gate_silu")
        ufull_ready = sem("ufull_ready")
        uhi_ready = sem("uhi_ready")
        u_ready = sem("u_ready")
        down_ready = sem("down_ready")
        y_added = sem("y_added")
        yt_zero = sem("yt_zero")
        out_stored = sem("out_stored")

        def after(order, turn, name):
            return turn * len(order) + (len(order) - order[::-1].index(name))

        lists = {at_pool_f: POOL_F, at_pool_b: POOL_B, at_act_f: ACT_F, at_act_b: ACT_B,
                 at_dve_f: DVE_F, at_dve_b: DVE_B, at_pe_f: PE_F, at_pe_b: PE_B}

        def event(s_, turn, name):
            return s_, after(lists[s_], turn, name) + (CREDIT if s_ is at_pool_b else 0)

        class Signals:

            def __init__(self, s_):
                self.s_, self.given = s_, []

            def __call__(self, name, i_):
                i_.then_inc(self.s_, 1)
                self.given.append(name)

            def close(self):
                assert self.given == lists[self.s_], self.given

        def attention_steps(eng, step):
            step(0, None, 0)
            with eng.Fori(1, TT - 2, 2) as i:
                step(i, i + (-1), 1)
                step(i + 1, i, 0)
            step(TT - 1, TT - 2, 1)
            step(None, TT - 1, 0)

        OUT_K = [4, 5, 6, 7, 0, 1, 2, 3]

        def turn_group(g):
            return g % KT, g // KT

        def out_pair(i):
            return pair[i + 2 if i < 2 else i % 2]

        def score_bank(n):
            return bank((0, 1, 7)[(n + 1) % 3])

        def ogc_count(turn, par):
            return 8 * (turn + (2 - par))

        passed = sem("passed")

        def apart(eng, *waits):
            for s_, n in waits:
                eng.wait_ge(s_, n)
            eng.sem_inc(passed, 1)

        block = ctx.enter_context(nc.Block())

        @block.sync
        def _(sp):
            a = lambda t, n: t.rearrange("l (r c) -> (l r) c", c=P)
            for row, name, n in ((ROW_C, "c", 8), (ROW_GPRE1, "g_pre_mix", 8), (ROW_GPOST1, "g_post_mix", 8),
                                 (ROW_GPRE2, "g_pre_ffn", 8), (ROW_GPOST2, "g_post_ffn", 8),
                                 (ROW_BADA, "b_ada", 48), (ROW_CB, "conv_b", 4), (ROW_LNG, "conv_ln_g", 4),
                                 (ROW_LNB, "conv_ln_b", 4), (ROW_LB, "hgrn_lower_bounds", 4),
                                 (ROW_NG, "hgrn_norm_g", 1)):
                sp.dma_start(rows_a[row:row + n, :], a(t_in[name], n)).then_inc(vec_loaded, 16)
            sp.dma_start(rows_b[:, :], t_in["conv_w"].rearrange("l j (t c) -> (l j t) c", c=P)).then_inc(vec_loaded, 16)
            for i in range(2):
                sp.dma_start(x0[:, 4 * i:4 * i + 4, :], x_d[:, 4 * i:4 * i + 4, :]).then_inc(x_loaded[i], 16)

            def load(g, src, ready):
                if ready is not None:
                    apart(sp, (w_split, ready))
                sp.dma_start(raw[:, g % RAW, :] if src.shape[1] != KT else
                             raw[:, g % RAW, :].rearrange("p (kt c) -> p kt c", kt=KT), src
                             ).then_inc(raw_loaded[g % RAW], 16)

            def in_tile(base, t):
                return w_in_d[:, :, ds(t * P + base * P, P)]

            def in_round(t, first):
                for j, base in enumerate((4, 0, 12, 8, 20, 16)):
                    load(j, in_tile(base, t), None if first and j < RAW else t * 6 + (j - 1))
            in_round(0, True)
            with sp.Fori(1, 4) as t:
                in_round(t, False)
            ahead = RAW + WS
            for n in range(ahead):
                load(N_IN + n, w_out_d[:, OUT_K[n]:OUT_K[n] + 1, :], N_IN + n - 1)
            sp.wait_ge(og_stored, 16 * HEADS + 16 * CREDIT)
            sp.wait_ge(v_ready, HEADS + CREDIT)
            for par in range(2):
                sp.dma_start(ogc[:, par], og_spill[:, :, par * P:(par + 1) * P]).then_inc(ogc_loaded[par], 16)
            with sp.Fori(2, TT - 1, 2) as c:
                for par in range(2):
                    apart(sp, event(at_dve_b, c + (par - 2), "MIX"))
                    sp.dma_start(ogc[:, par], og_spill[:, :, ds(c * P + par * P, P)]).then_inc(ogc_loaded[par], 16)
            sp.wait_ge(*event(at_pool_b, TT - 1, "LO"))
            sp.wait_ge(y_stored, 16 * CT + 16 * CREDIT)
            sp.dma_start(y4[:, :, :], y_spill).then_inc(y4_loaded, 16)
            for n in range(ahead, N_OUT):
                load(N_IN + n, w_out_d[:, OUT_K[n]:OUT_K[n] + 1, :], N_IN + n - 1)
            sp.wait_ge(ln_dve, LN_DVE)
            sp.dma_start(x1[:, :, :], x_d).then_inc(x1_loaded, 16)

            G0 = N_IN + N_OUT
            load(G0, w_up_d[:, :, 0:P], G0 - 1)
            load(G0 + 1, w_up_d[:, :, D_FF:D_FF + P], G0)

            def ffn_round(bk, last):
                g = G0 + 2
                srcs = [w_up_d[:, :, ds(bk * 2 * P + P, P)], w_up_d[:, :, ds(bk * 2 * P + P + D_FF, P)]]
                if not last:
                    srcs += [w_up_d[:, :, ds(bk * 2 * P + 2 * P, P)], w_up_d[:, :, ds(bk * 2 * P + 2 * P + D_FF, P)]]
                srcs += [w_down_d[:, ds(bk * 2, 1), :], w_down_d[:, ds(bk * 2 + 1, 1), :]]
                for j, src in enumerate(srcs):
                    load(g + j, src, bk * 6 + (g + j - 1))
            with sp.Fori(0, FB - 1) as bk:
                ffn_round(bk, False)
            ffn_round(FB - 1, True)
            for i in range(TT):
                if i < TT - 1:
                    sp.wait_ge(tail_done, TT + i + 1)
                else:
                    sp.wait_ge(last_done, 1)
                sp.dma_start(out_d[:, i, :], x1[:, i, :]).then_inc(out_stored, 16)
            sp.wait_ge(out_stored, 16 * TT)

        @block.gpsimd
        def _(pool):
            me = Tally(pool, pool_self)
            me.done(pool.memset(ident[:, :], 0.0))
            pool.memset(ones[:, :], 1.0).then_inc(consts_ready, 1)
            me.done(pool.memset(masks[:, :, :], 1.0))
            me.wait()
            pool.affine_select(out=ident[:, :], in_=ident[:, :], compare_op=ALU.not_equal, fill=1.0, base=0,
                               pattern=[[-1, P]], channel_multiplier=1).then_inc(consts_ready, 1)
            for n, size in enumerate(LEVELS):
                half, blocks = size // 2, P // size
                m = masks[:, n, :].rearrange("s (b h c) -> s b h c", h=2, c=half)
                me.done(pool.memset(m[:, :, 0, :], 0.0))
                right = m[:, :, 1, :]
                me.done(pool.affine_select(out=right, in_=right, compare_op=ALU.is_ge, fill=0.0, base=0,
                                           pattern=[[-size, blocks], [0, half]], channel_multiplier=1))
                me.wait()
                me.done(pool.affine_select(out=right, in_=right, compare_op=ALU.is_ge, fill=0.0, base=half - 1,
                                           pattern=[[size, blocks], [0, half]], channel_multiplier=-1))
            me.wait()
            pool.memset(lb_tmp[:, 4, :], 0.0).then_inc(consts_ready, 1)

            def split(j, loads, free, to=None):
                apart(pool, (raw_loaded[j % RAW], loads), *([(w_used, free)] if free is not None else []))
                hi, lo = to if to is not None else (w_hi[:, j % WS, :], w_lo[:, j % WS, :])
                src = raw[:, j % RAW, :]
                me.done(pool.tensor_copy(hi, src))
                me.wait()
                pool.tensor_tensor(lo, src, hi, ALU.subtract).then_inc(w_split, 1)

            for j in range(6):
                split(j, 16 * (j // RAW + 1), None if j < WS else j - WS + 1)
            def split_rounds(first, turns):
                r0 = first // 6
                with pool.Fori(r0, r0 + turns) as r:
                    me.enter(r + (-r0), 6)
                    for j in range(6):
                        split(j, r * 16 * (6 // RAW) + 16 * (j // RAW + 1), r * 6 + (j - WS + 1))
                me.leave(turns)

            def split_some(first, last):
                for g in range(first, last):
                    split(g % 6, 16 * (g // RAW + 1), g - WS + 1)
            split_rounds(6, 3)
            split_some(N_IN, N_IN + WS)

            def split_apart(n):
                g = N_IN + n
                split(g, 16 * (g // RAW + 1), None, (wo_hi[:, n - WS, :], wo_lo[:, n - WS, :]))

            pool.wait_ge(modt_summed, HEADS)
            me.done(pool.memset(pmat[:, :, :, :], 0.0))
            me.wait()
            pool.memset(state[:, 0, :, :], 0.0).then_inc(at_clear, 1)
            pool.wait_ge(b_ready, HEADS)
            pool.wait_ge(w_used, N_IN)

            def step(i, back, par):
                if i is not None:
                    signal = Signals(at_pool_f)
                    cols = ds(i * P, P)
                    if isinstance(i, int) and i == 0:
                        pass
                    else:
                        apart(pool, event(at_act_f, i - 1, "E5"))
                    bch = b[:, :, cols].rearrange("p h (g c) -> p h g c", c=CHUNK)
                    signal("DKD", pool.tensor_tensor(dd[:, 2].rearrange("p h (g c) -> p h g c", c=CHUNK), bch,
                                                     bch[:, :, :, CHUNK - 1:CHUNK].to_broadcast([P, HEADS, 2, CHUNK]),
                                                     ALU.subtract))

                    def diff(n):
                        size = LEVELS[n]
                        bv = b[:, :, cols].rearrange("p h (g c) -> p h g c", c=size)
                        ref = bv[:, :, :, size // 2 - 1:size // 2].to_broadcast([P, HEADS, P // size, size])
                        signal(f"D{n}", pool.tensor_tensor(dd[:, n % 3].rearrange("p h (g c) -> p h g c", c=size),
                                                           bv, ref, ALU.subtract))
                    diff(0)
                    apart(pool, event(at_act_f, i, "EKD"))
                    if not (isinstance(i, int) and i == 0):
                        apart(pool, event(at_pe_f, i - 1, "KDT"))
                    signal("KD", pool.tensor_tensor(kd[:, :, :], k[:, :, cols], ee[:, 2], ALU.mult))
                    apart(pool, event(at_act_f, i, "EB"))
                    signal("QE", pool.tensor_tensor(qe[:, par], q[:, :, cols], eb[:, :, :], ALU.mult))
                    for n in range(1, 6):
                        if n >= 3:
                            apart(pool, event(at_act_f, i, f"E{n - 3}"))
                        diff(n)
                    signal.close()
                else:
                    pool.wait_ge(*event(at_dve_f, back, "P5"))
                    split_apart(WS)
                if back is not None:
                    signal = Signals(at_pool_b)
                    cols = ds(back * P, P)
                    apart(pool, event(at_act_b, back, "HI"))
                    signal("LO", pool.tensor_tensor(hb_lo[:, :, cols], mixf[:, :, :], hb_hi[:, :, cols], ALU.subtract))
            pool.sem_inc(at_pool_b, CREDIT)
            attention_steps(pool, step)

            for n in range(WS + 1, N_OUT):
                split_apart(n)
            G0 = N_IN + N_OUT
            for g in range(G0, G0 + WS):
                split(g % 6, 16 * (g // RAW + 1), G0)
            pool.memset(yt[:, :, :], 0.0).then_inc(yt_zero, 1)
            first = -(-(G0 + WS) // 6) * 6
            split_some(G0 + WS, first)
            split_rounds(first, (N_CHUNKS - first) // 6)
            split_some(N_CHUNKS - N_CHUNKS % 6, N_CHUNKS)
            for i in range(TT - 1):
                pool.wait_ge(tail_read, TT + i + 1)
                pool.tensor_tensor(x1[:, i, :], x1[:, i, :], tail_tmp[:, i % 2, :], ALU.add).then_inc(tail_done, 1)

        @block.scalar
        def _(act):
            me = Tally(act, act_self)
            for s_ in (og_evac, vt_evac, v_ready):
                act.sem_inc(s_, CREDIT)
            for s_ in (og_stored, y_stored):
                act.sem_inc(s_, 16 * CREDIT)

            def root_mean_square(src, junk, col, which, count):
                me.done(act.activation(junk, src, ACT.Square, accum_out=ss[:, which, col:col + 1]))
                me.wait()
                return act.activation(rs[:, which, col:col + 1], ss[:, which, col:col + 1], ACT.Sqrt,
                                      scale=1.0 / count, bias=EPS)

            act.wait_ge(vec_ready, 2)
            act.activation(cond[:, :], vec[:, ROW_C:ROW_C + KT], ACT.Silu).then_inc(cond_ready, 1)
            for kt in range(3):
                act.dma_start(ada0[:, kt, :], w_ada_d[:, kt, 0:2 * D]).then_inc(ada0_loaded[kt], 16)
            act.activation(lb_tmp[:, 1, :], lb_tmp[:, 0, :], ACT.Exp).then_inc(cond_ready, 1)
            act.wait_ge(vec_ready, 3)
            act.activation(log_one_less_lb[:, :], one_less_lb[:, :], ACT.Ln).then_inc(cond_ready, 1)
            for i in range(TT):
                act.wait_ge(x_loaded[i // 4], 16)
                root_mean_square(x0[:, i, :], pair[2][:, :], i, 0, D).then_inc(ss_ready, 1)
            for kt in range(3, KT):
                act.wait_ge(ada0_used, kt - 2)
                act.dma_start(ada0[:, kt % 3, :], w_ada_d[:, kt, 0:2 * D]).then_inc(ada0_loaded[kt % 3], 16)

            def hi_parts(call, full, groups):
                for g in groups:
                    kt, half = turn_group(g)
                    act.wait_ge(full_ready, 16 * call + g + 1)
                    dst = (ha_hi if kt < 4 else hb_hi)[:, kt % 4, half * HALF:(half + 1) * HALF]
                    act.activation(dst, full[:, g % 2, :], ACT.Copy).then_inc(hi_ready, 1)
            hi_parts(0, full0, range(16))

            act.wait_ge(h_ready, 16)
            with act.Fori(0, 4) as t:
                me.enter(t, 3)

                def ada_loads(js):
                    for j in js:
                        act.wait_ge(ada_used, t * KT + max(0, j - 1) + CREDIT)
                        act.dma_start(ada[:, j % 2, :], w_ada_d[:, j, ds(t * D + 2 * D, D)]
                                      ).then_inc(ada_loaded[j % 2], 16)
                ada_loads(range(5))
                act.wait_ge(w_used, t * 6 + 1)
                act.wait_ge(u_evac, t + CREDIT)
                act.activation(sg[:, :], pair[0][:, :], ACT.Sigmoid).then_inc(gate_sig, 1)
                ada_loads(range(5, KT))
                apart(act, (w_used, t * 6 + 3))
                me.done(act.activation(k[:, t, :], pair[0][:, :], ACT.Sigmoid, scale=-1.0))
                me.done(act.activation(b[:, t, :], pair[0][:, :], ACT.Abs))
                apart(act, me.last())
                me.done(act.activation(b[:, t, :], b[:, t, :], ACT.Exp, scale=-1.0))
                apart(act, me.last())
                act.activation(b[:, t, :], b[:, t, :], ACT.Ln, bias=1.0).then_inc(z_log, 1)
                apart(act, (w_used, t * 6 + 4))
                act.activation(q[:, t, :], pair[1][:, :], ACT.Silu).then_inc(q_evac, 1)
                act.wait_ge(w_used, t * 6 + 5)
                act.wait_ge(og_stored, t * 16 + 16 * CREDIT)
                act.activation(ogt[:, :], pair[0][:, :], ACT.Silu).then_inc(og_evac, 1)
                act.wait_ge(og_evac, t + 1 + CREDIT)
                act.dma_start(og_spill[:, t, :], ogt[:, :]).then_inc(og_stored, 16)
                act.wait_ge(w_used, t * 6 + 6)
                act.activation(vt[:, :], pair[1][:, :], ACT.Copy).then_inc(vt_evac, 1)
                apart(act, (v_turned, t + 1))
                act.activation(v[:, :, ds(t * P, P)], pair[2][:, :].rearrange("s (c n) -> s c n", n=P),
                               ACT.Copy).then_inc(v_ready, 1)
                act.wait_ge(tap_done, t * 2 * TAPS + 2 * TAPS + CREDIT)
                act.dma_start(y_spill[:, t, :], y[:, :]).then_inc(y_stored, 16)
            me.leave(4)

            act.wait_ge(b_ready, HEADS)
            act.wait_ge(v_ready, HEADS + CREDIT)

            def step(i, back, par):
                if i is not None:
                    first = isinstance(i, int) and i == 0
                    signal = Signals(at_act_f)
                    cols = ds(i * P, P)
                    if not first:
                        apart(act, event(at_pe_f, i - 1, "DIAG"))
                    signal("KC", act.activation(kc[:, :, :], k[:, :, cols], ACT.Copy))
                    signal("VC", act.activation(vc[:, par], v[:, i, :].rearrange("s (h n) -> s h n", n=P), ACT.Copy))
                    act.wait_ge(*event(at_pool_f, i, "DKD"))
                    if not first:
                        act.wait_ge(*event(at_dve_f, i - 1, "ST0"))
                    signal("EKD", act.activation(ee[:, 2], dd[:, 2], ACT.Exp, scale=-1.0))
                    signal("EB", act.activation(eb[:, :, :], b[:, :, cols], ACT.Exp))

                    def decay(n):
                        act.wait_ge(*event(at_pool_f, i, f"D{n}"))
                        if n >= 3:
                            act.wait_ge(*event(at_dve_f, i, f"X{n - 3}"))
                        dv, ev = (w[:, n % 3].rearrange("p h (g s c) -> p (h g) s c", s=2, c=LEVELS[n] // 2)
                                  for w in (dd, ee))
                        signal(f"EL{n}", act.activation(ev[:, :, 0, :], dv[:, :, 0, :], ACT.Exp, scale=-1.0))
                        signal(f"E{n}", act.activation(ev[:, :, 1, :], dv[:, :, 1, :], ACT.Exp))
                    decay(0)
                if back is not None:
                    signal_b = Signals(at_act_b)
                    act.wait_ge(*event(at_pe_b, back, "O"))
                    signal_b("SQ", act.activation(sq[:, :, :], bank(5).rearrange("s (h n) -> s h n", n=P), ACT.Square))
                if i is not None:
                    decay(1)
                    act.wait_ge(*event(at_pe_f, i, "KDT"))
                    signal("KDT", act.activation(kdt[:, :, :], bank(2).rearrange("s (h n) -> s h n", n=P), ACT.Copy))
                if back is not None:
                    act.wait_ge(*event(at_dve_b, back, "SS"))
                    signal_b("LN", act.activation(rs[:, 2, 0:4], ss[:, 2, 0:4], ACT.Ln, scale=1.0 / P, bias=EPS))
                    act.wait_ge(*event(at_act_b, back, "LN"))
                    signal_b("RSTD", act.activation(rs[:, 2, 4:8], rs[:, 2, 0:4], ACT.Exp, scale=-0.5))
                if i is not None:
                    for n in range(2, 6):
                        decay(n)
                    signal.close()
                if back is not None:
                    apart(act, event(at_dve_b, back, "MIX"))
                    signal_b("HI", act.activation(hb_hi[:, :, ds(back * P, P)], mixf[:, :, :], ACT.Copy))
                    signal_b.close()
            attention_steps(act, step)

            for t in range(CT):
                act.wait_ge(ln_dve, t + 1)
                if t >= 2:
                    act.wait_ge(ln_pe, 1 + t - 1)
                act.activation(ln_sq[:, t % 2, :], y4[:, t, :], ACT.Square).then_inc(ln_act, 1)
            act.wait_ge(ln_pe, 1 + CT)
            me.done(act.activation(ln_rs[:, :], pair[1][:, :], ACT.Ln, scale=1.0 / (CT * P), bias=EPS))
            me.wait()
            act.activation(ln_rs[:, :], ln_rs[:, :], ACT.Exp, scale=-0.5).then_inc(ln_act, 1)
            for t in range(CT):
                act.wait_ge(ln_dve, CT + t + 1 + max(0, t - 1))
                act.activation(ln_f[:, t % 2, :], y4[:, t, :], ACT.Silu, scale=vec[:, ROW_LNG + t:ROW_LNG + t + 1],
                               bias=vec[:, ROW_LNB + t:ROW_LNB + t + 1]).then_inc(ln_act, 1)
                act.wait_ge(ln_act, CT + 1 + 2 * t + 1)
                act.activation(ha_hi[:, t, :], ln_f[:, t % 2, :], ACT.Copy).then_inc(ln_act, 1)

            def tail_norm(src, slot, i):
                root_mean_square(src, tail_tmp[:, slot, :], i, 1, D).then_inc(tail_ss, 1)

            def x1_norm(i):
                act.wait_ge(tail_done, i + 1)
                root_mean_square(x1[:, i, :], tail_tmp[:, 1, :], i, 3, D).then_inc(x1_ss, 1)
            for i in range(TT):
                act.wait_ge(w_used, N_IN + i + 1)
                tail_norm(out_pair(i)[:, :], 1, i)
                x1_norm(i)
                if i in (4, 5):
                    hi_parts(1, full1, range(4 * (i - 4), 4 * (i - 3)))
            hi_parts(1, full1, range(8, 16))

            F0 = N_IN + N_OUT

            def silu_gate(e, used, first=False):
                act.wait_ge(w_used, used)
                if not first:
                    act.wait_ge(ufull_ready, e)
                act.activation(gate[:, :], pair[0][:, :], ACT.Silu).then_inc(gate_silu, 1)

            def u_hi_part(e, slot):
                act.wait_ge(ufull_ready, e + 1)
                act.activation(u_hi[:, slot, :], ufull[:, :], ACT.Copy).then_inc(uhi_ready, 1)
            act.wait_ge(h_ready, 32)
            silu_gate(0, F0 + 1, first=True)
            u_hi_part(0, 0)
            with act.Fori(0, FB - 1) as bk:
                silu_gate(bk * 2 + 1, bk * 6 + (F0 + 3))
                u_hi_part(bk * 2 + 1, 1)
                silu_gate(bk * 2 + 2, bk * 6 + (F0 + 5))
                act.wait_ge(w_used, bk * 6 + (F0 + 8))
                u_hi_part(bk * 2 + 2, 0)
            silu_gate(FFT - 1, 6 * (FB - 1) + F0 + 3)
            u_hi_part(FFT - 1, 1)
            for i in range(TT):
                act.wait_ge(y_added, (FB - 1) * TT + i + 1 + CREDIT)
                if i >= 2:
                    act.wait_ge(tail_done, TT + i - 1)
                tail_norm(yt[:, i, :], i % 2, i)

        @block.vector
        def _(dve):
            me = Tally(dve, dve_self)
            for s_ in (tap_done, ada_used, modt_ready, y_added, u_evac):
                dve.sem_inc(s_, CREDIT)
            me.done(dve.memset(scan_keep[:, :], 1.0))
            me.wait()
            me.done(dve.memset(scan_keep[:, 0:S:CHUNK], 0.0))
            dve.wait_ge(vec_turned, 1)
            dve.tensor_copy(vec[:, :], pair[3][:, 0:ROWS]).then_inc(vec_ready, 1)
            me.done(dve.tensor_copy(conv_w_col[:, :], pair[3][:, P:P + TAPS * CT]))
            dve.wait_ge(vec_ready, 1)
            lbv = vec[:, ROW_LB:ROW_LB + HEADS]
            dve.tensor_tensor(lb_tmp[:, 0, :], lbv, lbv, ALU.subtract).then_inc(vec_ready, 1)
            dve.wait_ge(cond_ready, 2)
            me.done(dve.reciprocal(lb_tmp[:, 2, :], lb_tmp[:, 1, :]))
            me.wait()
            me.done(dve.tensor_tensor(lb_tmp[:, 3, :], lb_tmp[:, 1, :], lb_tmp[:, 2, :], ALU.mult))
            me.wait()
            me.done(dve.tensor_tensor(lb_tmp[:, 2, :], lb_tmp[:, 3, :], lb_tmp[:, 3, :], ALU.subtract))
            me.wait()
            dve.tensor_scalar(one_less_lb[:, :], lb_tmp[:, 2, :], -1.0, 1.0, ALU.mult, ALU.add).then_inc(vec_ready, 1)

            def normalise(dst, src, col, which):
                me.done(dve.reciprocal(rs[:, which, col:col + 1], rs[:, which, col:col + 1]))
                me.wait()
                return dve.tensor_scalar(dst, src, rs[:, which, col:col + 1], None, ALU.mult)

            for kt in range(KT):
                dve.wait_ge(ada0_loaded[kt % 3], 16 * (kt // 3 + 1))
                if kt == 0:
                    dve.wait_ge(cond_ready, 1)
                    i_ = dve.tensor_scalar(acc0[:, :], ada0[:, 0, :], cond[:, 0:1], None, ALU.mult)
                else:
                    dve.wait_ge(ada0_used, kt)
                    i_ = dve.scalar_tensor_tensor(out=acc0[:, :], in0=ada0[:, kt % 3, :], scalar=cond[:, kt:kt + 1],
                                                  in1=acc0[:, :], op0=ALU.mult, op1=ALU.add)
                i_.then_inc(ada0_used, 1)
                dve.wait_ge(ss_ready, kt + 1)
                normalise(x0[:, kt, :], x0[:, kt, :], kt, 0).then_inc(xs_ready, 1)
            dve.wait_ge(mod0_summed, 1)
            me.done(dve.tensor_tensor(mod[:, 0:16], pair[3][:, 256:272], vec[:, ROW_BADA:ROW_BADA + 16], ALU.add))
            me.wait()
            dve.scalar_tensor_tensor(out=gs[:, 0, :], in0=mod[:, 8:16], scalar=1.0,
                                     in1=vec[:, ROW_GPRE1:ROW_GPRE1 + KT], op0=ALU.add, op1=ALU.mult).then_inc(mod_ready, 1)
            dve.wait_ge(mod_ready, 1)

            def modulate(call, full, shift, groups):
                def lo(g):
                    kt, half = turn_group(g)
                    dve.wait_ge(hi_ready, 16 * call + g + 1)
                    cols = slice(half * HALF, (half + 1) * HALF)
                    hi = (ha_hi if kt < 4 else hb_hi)[:, kt % 4, cols]
                    dve.tensor_tensor((ha_lo if kt < 4 else hb_lo)[:, kt % 4, cols], full[:, g % 2, :], hi,
                                      ALU.subtract).then_inc(h_ready, 1)
                for g in groups:
                    kt, half = turn_group(g)
                    dve.wait_ge(turned, 16 * call + g + 1)
                    if g >= 2:
                        dve.wait_ge(h_ready, 16 * call + g - 1)
                    dve.tensor_scalar(full[:, g % 2, :], bank(4 * call + g % 4), gs[:, call, kt:kt + 1],
                                      mod[:, shift + kt:shift + kt + 1], ALU.mult, ALU.add).then_inc(full_ready, 1)
                    if g > groups[0]:
                        lo(g - 1)
                lo(groups[-1])
            modulate(0, full0, 0, range(16))

            dve.wait_ge(h_ready, 16)
            me.done(dve.memset(u[:, 0:TAPS - 1], 0.0))
            IN_DVE = 4 + 2
            cwv = conv_w_col[:, :].rearrange("p (j t) -> p j t", t=CT)
            with dve.Fori(0, 4) as t:
                me.enter(t, IN_DVE)
                dve.wait_ge(tap_done, t * 2 * TAPS + CREDIT)
                me.wait()
                me.done(dve.tensor_copy(tile_w[:, :], cwv[:, :, t]))
                me.done(dve.tensor_copy(tile_cols[:, 0:1], vec[:, ds(t + ROW_CB, 1)]))
                me.done(dve.tensor_copy(tile_cols[:, 1:2], one_less_lb[:, ds(t, 1)]))
                me.done(dve.tensor_copy(lb_tmp[:, 0, 0:1], log_one_less_lb[:, ds(t, 1)]))
                for j in range(KT):
                    dve.wait_ge(ada_loaded[j % 2], t * 16 * (KT // 2) + 16 * (j // 2 + 1))
                    if j == 0:
                        i_ = dve.tensor_scalar(acc[:, :], ada[:, 0, :], cond[:, 0:1], None, ALU.mult)
                    else:
                        dve.wait_ge(ada_used, t * KT + j + CREDIT)
                        i_ = dve.scalar_tensor_tensor(out=acc[:, :], in0=ada[:, j % 2, :], scalar=cond[:, j:j + 1],
                                                      in1=acc[:, :], op0=ALU.mult, op1=ALU.add)
                    i_.then_inc(ada_used, 1)
                me.wait()
                dve.wait_ge(gate_sig, t + 1)
                dve.wait_ge(w_used, t * 6 + 2)
                dve.tensor_tensor(u[:, TAPS - 1:], sg[:, :], pair[1][:, :], ALU.mult).then_inc(u_evac, 1)
                dve.wait_ge(u_evac, t + 1 + CREDIT)
                dve.wait_ge(y_stored, t * 16 + 16 * CREDIT)

                def taps(lo, hi):
                    for j in range(lo, hi):
                        for h in range(2):
                            dst = y[:, h * HALF:(h + 1) * HALF]
                            src = u[:, h * HALF + j:h * HALF + j + HALF]
                            if j == 0:
                                i_ = dve.tensor_scalar(dst, src, tile_w[:, 0:1], tile_cols[:, 0:1], ALU.mult, ALU.add)
                            else:
                                dve.wait_ge(tap_done, t * 2 * TAPS + (2 * j + h - 1) + CREDIT)
                                i_ = dve.scalar_tensor_tensor(out=dst, in0=src, scalar=tile_w[:, j:j + 1], in1=dst,
                                                              op0=ALU.mult, op1=ALU.add)
                            i_.then_inc(tap_done, 1)
                taps(0, 11)
                dve.wait_ge(z_log, t + 1)
                dve.scalar_tensor_tensor(out=b[:, t, :], in0=pair[0][:, :], scalar=0.0, in1=b[:, t, :],
                                         op0=ALU.min, op1=ALU.subtract).then_inc(z_evac, 1)
                dve.wait_ge(z_evac, t + 1)
                me.done(dve.tensor_scalar(b[:, t, :], b[:, t, :], lb_tmp[:, 0, 0:1], None, ALU.add))
                me.done(dve.tensor_scalar(k[:, t, :], k[:, t, :], tile_cols[:, 1:2], None, ALU.mult))
                me.wait()
                dve.tensor_tensor_scan(b[:, t, :], scan_keep[:, :], b[:, t, :], 0.0, ALU.mult, ALU.add).then_inc(b_ready, 1)
                taps(11, TAPS)
                dve.wait_ge(modt_summed, t + 1)
                dve.tensor_tensor(mod[:, ds(t * KT + 16, KT)], pair[3][:, 288:288 + KT],
                                  vec[:, ds(t * KT + (ROW_BADA + 16), KT)], ALU.add).then_inc(modt_ready, 1)
            me.leave(4)
            dve.wait_ge(modt_ready, 4 + CREDIT)
            dve.scalar_tensor_tensor(out=gs[:, 1, :], in0=mod[:, 32:40], scalar=1.0,
                                     in1=vec[:, ROW_GPRE2:ROW_GPRE2 + KT], op0=ALU.add, op1=ALU.mult).then_inc(mod_ready, 1)
            dve.tensor_tensor(gg[:, 0, :], mod[:, 16:24], vec[:, ROW_GPOST1:ROW_GPOST1 + KT], ALU.mult).then_inc(mod_ready, 1)
            dve.tensor_tensor(gg[:, 1, :], mod[:, 40:48], vec[:, ROW_GPOST2:ROW_GPOST2 + KT], ALU.mult).then_inc(mod_ready, 1)

            me.wait()
            dve.wait_ge(w_used, N_IN)
            dve.wait_ge(v_ready, HEADS + CREDIT)
            dve.wait_ge(b_ready, HEADS)
            dve.wait_ge(consts_ready, 3)
            dve.wait_ge(at_clear, 1)

            def step(i, back, par):
                def on_front(s_, name):
                    dve.wait_ge(*event(s_, i, name))
                if i is not None:
                    signal = Signals(at_dve_f)
                    cols = ds(i * P, P)
                if back is not None:
                    signal_b = Signals(at_dve_b)

                def scaled(n):
                    if i is None:
                        return
                    on_front(at_act_f, f"E{n}")
                    ev, xv, kv, qv = (w.rearrange("p h (g s c) -> p h g s c", s=2, c=LEVELS[n] // 2)
                                      for w in (ee[:, n % 3], xr[:, n % 3], k[:, :, cols], q[:, :, cols]))
                    signal(f"XL{n}", dve.tensor_tensor(xv[:, :, :, 0, :], kv[:, :, :, 0, :], ev[:, :, :, 0, :], ALU.mult))
                    signal(f"X{n}", dve.tensor_tensor(xv[:, :, :, 1, :], qv[:, :, :, 1, :], ev[:, :, :, 1, :], ALU.mult))

                def place(n):
                    if i is None:
                        return
                    waits = [event(at_pe_f, i, f"S{n}" if n >= 0 else "DIAG")]
                    if n >= 0:
                        waits.append(event(at_dve_f, i, f"P{n - 1}" if n else "PD"))
                    apart(dve, *waits)
                    mask = masks[:, n, :] if n >= 0 else ident[:, :]
                    signal(f"P{n}" if n >= 0 else "PD",
                           dve.copy_predicated(pmat[:, par], mask.bitcast(I32).unsqueeze(1).to_broadcast([P, HEADS, P]),
                                               score_bank(n).rearrange("s (h n) -> s h n", n=P)))
                scaled(0)
                if back is not None:
                    dve.wait_ge(*event(at_act_b, back, "SQ"))
                    signal_b("SS", dve.tensor_reduce(ss[:, 2, 0:4], sq[:, :, :], AX_X, ALU.add))
                scaled(1)
                place(-1)
                place(0)
                if back is not None:
                    dve.wait_ge(*event(at_act_b, back, "RSTD"))
                    signal_b("ON", dve.tensor_tensor(on[:, :, :], bank(5).rearrange("s (h n) -> s h n", n=P),
                                                     rs[:, 2, 4:8].unsqueeze(2).to_broadcast([P, HEADS, P]), ALU.mult))
                scaled(2)
                place(1)
                scaled(3)
                place(2)
                if back is not None:
                    dve.wait_ge(*event(at_pe_b, back, "OT"))
                    dve.wait_ge(ogc_loaded[1 - par], ogc_count(back, 1 - par))
                    if not (isinstance(back, int) and back == 0):
                        dve.wait_ge(*event(at_pool_b, back - 1, "LO"))
                    signal_b("MIX", dve.scalar_tensor_tensor(
                        out=mixf[:, :, :], in0=bank(6).rearrange("p (h n) -> p h n", n=P),
                        scalar=vec[:, ROW_NG:ROW_NG + 1], in1=ogc[:, 1 - par], op0=ALU.mult, op1=ALU.mult))
                    signal_b.close()
                scaled(4)
                place(3)
                scaled(5)
                place(4)
                if i is not None:
                    for j in range(2):
                        on_front(at_pe_f, f"C{j}")
                        if j:
                            on_front(at_dve_f, "ST1")
                        elif not (isinstance(i, int) and i == 0):
                            dve.wait_ge(*event(at_dve_f, i - 1, "ST0"))
                        last = CHUNK * (j + 1) - 1
                        for h in range(HEADS):
                            signal("ST0" if j else "ST1", dve.scalar_tensor_tensor(
                                out=state[:, (2 * par + j + 1) % 4, h, :], in0=state[:, 2 * par + j, h, :],
                                scalar=eb[:, h, last:last + 1], in1=bank(3 + j)[:, h * P:(h + 1) * P],
                                op0=ALU.mult, op1=ALU.add))
                    place(5)
                    signal.close()
            attention_steps(dve, step)

            dve.wait_ge(ggb_pe, 1)
            dve.tensor_copy(ggb[:, :], pair[3][:, :]).then_inc(ggb_ready, 1)
            dve.wait_ge(ln_pe, 1)
            for t in range(CT):
                dve.scalar_tensor_tensor(out=y4[:, t, :], in0=pair[0][:, :], scalar=-1.0 / (CT * P), in1=y4[:, t, :],
                                         op0=ALU.mult, op1=ALU.add).then_inc(ln_dve, 1)
            dve.wait_ge(ln_act, CT + 1)

            def ln_lo(t):
                dve.wait_ge(ln_act, CT + 1 + 2 * (t + 1))
                dve.tensor_tensor(ha_lo[:, t, :], ln_f[:, t % 2, :], ha_hi[:, t, :], ALU.subtract).then_inc(ln_dve, 1)
            for t in range(CT):
                dve.tensor_tensor(y4[:, t, :], y4[:, t, :], ln_rs[:, :], ALU.mult).then_inc(ln_dve, 1)
                if t:
                    ln_lo(t - 1)
            ln_lo(CT - 1)

            def scaled_product(i, src, slot, count):
                dve.wait_ge(tail_ss, count)
                me.done(dve.reciprocal(rs[:, 1, i:i + 1], rs[:, 1, i:i + 1]))
                me.wait()
                dve.scalar_tensor_tensor(out=tail_tmp[:, slot, :], in0=src, scalar=rs[:, 1, i:i + 1], in1=ggb[:, :],
                                         op0=ALU.mult, op1=ALU.mult).then_inc(tail_read, 1)

            def residual(i):
                scaled_product(i, out_pair(i)[:, :], 1, i + 1)
                dve.wait_ge(tail_read, i + 1)
                dve.tensor_tensor(x1[:, i, :], x1[:, i, :], tail_tmp[:, 1, :], ALU.add).then_inc(tail_done, 1)

            def next_norm(i):
                dve.wait_ge(x1_ss, i + 1)
                if i >= 4:
                    dve.wait_ge(turned, 16 + 8)
                normalise(xs[:, i % 4, :], x1[:, i, :], i, 3).then_inc(xs_ready, 1)
            dve.wait_ge(x1_loaded, 16)
            for i in range(TT):
                residual(i)
                if i in (4, 5):
                    modulate(1, full1, 24, range(4 * (i - 4), 4 * (i - 3)))
                if i != 4:
                    for n in (4, 5) if i == 5 else (i,):
                        next_norm(n)
            modulate(1, full1, 24, range(8, 16))


            def u_full(e, used, first=False):
                dve.wait_ge(gate_silu, e + 1)
                dve.wait_ge(w_used, used)
                if not first:
                    dve.wait_ge(u_ready, e)
                dve.tensor_tensor(ufull[:, :], gate[:, :], pair[1][:, :], ALU.mult).then_inc(ufull_ready, 1)

            def u_low(e, slot):
                dve.wait_ge(uhi_ready, e + 1)
                dve.tensor_tensor(u_lo[:, slot, :], ufull[:, :], u_hi[:, slot, :], ALU.subtract).then_inc(u_ready, 1)

            def add_tile(bk, i, used):
                if i < TT - 1:
                    dve.wait_ge(down_ready, bk * (TT - 1) + (i + 1))
                else:
                    dve.wait_ge(w_used, used)
                dve.tensor_tensor(yt[:, i, :], yt[:, i, :], pair[2 + i % 2][:, :], ALU.add).then_inc(y_added, 1)

            def add_down(bk, used):
                for i in range(TT):
                    add_tile(bk, i, used)
            F0 = N_IN + N_OUT
            u_full(0, F0 + 2, first=True)
            u_low(0, 0)
            dve.wait_ge(yt_zero, 1)
            with dve.Fori(0, FB - 1) as bk:
                u_full(bk * 2 + 1, bk * 6 + (F0 + 4))
                u_low(bk * 2 + 1, 1)
                u_full(bk * 2 + 2, bk * 6 + (F0 + 6))
                add_down(bk, bk * 6 + (F0 + 8))
                u_low(bk * 2 + 2, 0)
            u_full(FFT - 1, 6 * (FB - 1) + F0 + 4)
            u_low(FFT - 1, 1)
            dve.wait_ge(ggb_pe, 2)
            dve.tensor_copy(ggb[:, :], pair[0][:, :]).then_inc(ggb_ready, 1)
            dve.wait_ge(ggb_ready, 2)
            for i in range(TT + 1):
                if i < TT:
                    add_tile(FB - 1, i, 6 * (FB - 1) + F0 + 6)
                if i:
                    scaled_product(i - 1, yt[:, i - 1, :], (i - 1) % 2, TT + i)
            dve.wait_ge(tail_read, 2 * TT)
            dve.tensor_tensor(x1[:, TT - 1, :], x1[:, TT - 1, :], tail_tmp[:, (TT - 1) % 2, :], ALU.add
                              ).then_inc(last_done, 1)

        @block.tensor
        def _(pe):
            pe.wait_ge(consts_ready, 2)
            pe.wait_ge(vec_loaded, 16 * VEC_LOADS)
            pe.transpose(pair[3][:, 0:ROWS], rows_a[:, :], ident[0:ROWS, 0:ROWS])
            pe.transpose(pair[3][:, P:P + TAPS * CT], rows_b[:, :], ident[0:TAPS * CT, 0:TAPS * CT]).then_inc(vec_turned, 1)

            def column_sums(src, dst, tiles):
                for n in range(tiles):
                    i_ = pe.matmul(dst[:, n:n + 1], src[:, n * P:(n + 1) * P], ones[:, 0:1], start=True, stop=True)
                return i_
            pe.wait_ge(ada0_used, KT)
            pe.wait_ge(vec_ready, 2)
            column_sums(acc0, pair[3][:, 256:272], 16).then_inc(mod0_summed, 1)

            def turn_tiles(call, src, groups):
                for g in groups:
                    kt, half = turn_group(g)
                    if g >= 4:
                        pe.wait_ge(full_ready, 16 * call + g - 3)
                    for i in range(4):
                        tile = 4 * half + i
                        pe.wait_ge(xs_ready, TT * call + tile + 1)
                        i_ = pe.transpose(bank(4 * call + g % 4)[:, i * P:(i + 1) * P],
                                          src[:, tile % src.shape[1], kt * P:(kt + 1) * P], ident[:, :])
                    i_.then_inc(turned, 1)
            turn_tiles(0, x0, range(16))

            def split_product(dst, slot, w_cols, x_hi, x_lo, first, last):
                wh, wl = w_hi[:, slot, w_cols], w_lo[:, slot, w_cols]
                steps = [(wh, x_hi), (wh, x_lo), (wl, x_hi)]
                for s_, (w, x) in enumerate(steps):
                    for half in range(2):
                        cols = slice(half * HALF, (half + 1) * HALF)
                        i_ = pe.matmul(dst[:, cols], w, x[:, cols], start=first and s_ == 0, stop=last and s_ == 2)
                return i_

            def project(dst, slot):
                for kt in range(KT):
                    hi, lo = (ha_hi, ha_lo) if kt < 4 else (hb_hi, hb_lo)
                    i_ = split_product(dst, slot, slice(kt * P, (kt + 1) * P), hi[:, kt % 4, :], lo[:, kt % 4, :],
                                       kt == 0, kt == KT - 1)
                return i_

            pe.wait_ge(h_ready, 16)
            with pe.Fori(0, 4) as t:
                free = [(og_evac, t + CREDIT), (vt_evac, t + CREDIT), (gate_sig, t + 1), (u_evac, t + 1 + CREDIT), (z_evac, t + 1), (q_evac, t + 1)]
                for j in range(6):
                    pe.wait_ge(w_split, t * 6 + (j + 1))
                    pe.wait_ge(*free[j])
                    project(pair[j % 2], j % WS).then_inc(w_used, 1)
                    if j == 2:
                        pe.wait_ge(ada_used, t * KT + KT + CREDIT)
                        pe.wait_ge(modt_ready, t + CREDIT)
                        column_sums(acc, pair[3][:, 288:288 + KT], KT).then_inc(modt_summed, 1)
                pe.wait_ge(vt_evac, t + 1 + CREDIT)
                pe.wait_ge(v_ready, t + CREDIT)
                for c in range(TT):
                    i_ = pe.transpose(pair[2][:, c * P:(c + 1) * P], vt[:, c * P:(c + 1) * P], ident[:, :])
                i_.then_inc(v_turned, 1)

            pe.wait_ge(modt_ready, 4 + CREDIT)
            pe.wait_ge(v_ready, 4 + CREDIT)

            def step(i, back, par):
                def on_front(s_, name):
                    pe.wait_ge(*event(s_, i, name))
                if back is not None:
                    signal_b = Signals(at_pe_b)
                    bp = 1 - par
                    pe.wait_ge(*event(at_pool_f, back, "QE"))
                    pe.wait_ge(*event(at_dve_f, back, "P5"))
                    for h in range(HEADS):
                        o = bank(5)[:, h * P:(h + 1) * P]
                        pe.matmul(o, pmat[:, bp, h, :], vc[:, bp, h, :], start=True, stop=False, skip_group_check=True)
                        for j in range(2):
                            rows = slice(j * CHUNK, (j + 1) * CHUNK)
                            i_ = pe.matmul(o[rows, :], qe[:, bp, h, rows], state[:, 2 * bp + j, h, :], start=False,
                                           stop=True, skip_group_check=True)
                    signal_b("O", i_)
                if i is not None:
                    signal = Signals(at_pe_f)
                    on_front(at_pool_f, "KD")
                    for h in range(HEADS):
                        i_ = pe.transpose(bank(2)[:, h * P:(h + 1) * P], kd[:, h, :], ident[:, :])
                    signal("KDT", i_)
                    on_front(at_act_f, "KC")
                    for h in range(HEADS):
                        i_ = pe.matmul(score_bank(-1)[:, h * P:(h + 1) * P], kc[:, h, :], q[:, h, ds(i * P, P)],
                                       start=True, stop=True)
                    signal("DIAG", i_)
                    for n in range(len(LEVELS)):
                        on_front(at_dve_f, f"X{n}")
                        if n >= 2:
                            on_front(at_dve_f, "PD" if n == 2 else f"P{n - 3}")
                        for h in range(HEADS):
                            i_ = pe.matmul(score_bank(n)[:, h * P:(h + 1) * P], xr[:, n % 3, h, :], xr[:, n % 3, h, :],
                                           start=True, stop=True)
                        signal(f"S{n}", i_)
                        if n == 1 and back is not None:
                            turn_output(back, signal_b)
                        if n == 2:
                            on_front(at_act_f, "KDT")
                            for j in range(2):
                                rows = slice(j * CHUNK, (j + 1) * CHUNK)
                                for h in range(HEADS):
                                    i_ = pe.matmul(bank(3 + j)[:, h * P:(h + 1) * P], kdt[rows, h, :], vc[rows, par, h, :],
                                                   start=True, stop=True)
                                signal(f"C{j}", i_)
                    signal.close()
                elif back is not None:
                    turn_output(back, signal_b)

            def turn_output(back, signal_b):
                pe.wait_ge(*event(at_dve_b, back, "ON"))
                for h in range(HEADS):
                    i_ = pe.transpose(bank(6)[:, h * P:(h + 1) * P], on[:, h, :], ident[:, :])
                signal_b("OT", i_)
                signal_b.close()
            attention_steps(pe, step)

            def gg_rows(call, dst):
                for n in range(KT):
                    i_ = pe.matmul(dst[:, n * P:(n + 1) * P], gg[:, call, n:n + 1].to_broadcast([P, P]), ident[:, :],
                                   start=True, stop=True)
                i_.then_inc(ggb_pe, 1)
            pe.wait_ge(mod_ready, 4)
            pe.wait_ge(*event(at_pool_b, TT - 1, "LO"))
            gg_rows(0, pair[3])

            def token_product(dst, x_hi, x_lo, wh, wl, first, last):
                for s_, (x, w) in enumerate([(x_hi, wh), (x_hi, wl), (x_lo, wh)]):
                    for half in range(2):
                        cols = slice(half * HALF, (half + 1) * HALF)
                        i_ = pe.matmul(dst[:, cols], x, w[:, cols], start=first and s_ == 0, stop=last and s_ == 2)
                return i_

            def out_tile(i, steps):
                tokens = slice(i * P, (i + 1) * P)
                for n in steps:
                    if i == 0:
                        pe.wait_ge(w_split, N_IN + n + 1)
                    kt = OUT_K[n]
                    hi, lo = (ha_hi, ha_lo) if kt < 4 else (hb_hi, hb_lo)
                    g = N_IN + n
                    wh, wl = ((w_hi[:, g % WS, :], w_lo[:, g % WS, :]) if n < WS else
                              (wo_hi[:, n - WS, :], wo_lo[:, n - WS, :]))
                    i_ = token_product(out_pair(i), hi[:, kt % 4, tokens], lo[:, kt % 4, tokens], wh, wl,
                                       n == 0, n == N_OUT - 1)
                return i_

            pe.wait_ge(y4_loaded, 16)
            for t in range(CT):
                for half in range(2):
                    cols = slice(half * HALF, (half + 1) * HALF)
                    i_ = pe.matmul(pair[0][:, cols], ones[:, :], y4[:, t, cols], start=t == 0, stop=t == CT - 1)
            i_.then_inc(ln_pe, 1)
            out_tile(0, range(4))
            for t in range(CT):
                pe.wait_ge(ln_act, t + 1)
                for half in range(2):
                    cols = slice(half * HALF, (half + 1) * HALF)
                    i_ = pe.matmul(pair[1][:, cols], ones[:, :], ln_sq[:, t % 2, cols], start=t == 0, stop=t == CT - 1)
                i_.then_inc(ln_pe, 1)

            pe.wait_ge(ggb_ready, 1)
            out_tile(1, range(4))
            pe.wait_ge(ln_dve, LN_DVE)
            for i in range(TT):
                if i >= 4:
                    pe.wait_ge(tail_read, i - 1)
                out_tile(i, range(4 if i < 2 else 0, N_OUT)).then_inc(w_used, 1)
                if i in (4, 5):
                    turn_tiles(1, xs, range(4 * (i - 4), 4 * (i - 3)))
            turn_tiles(1, xs, range(8, 16))

            pe.wait_ge(h_ready, 32)
            F0 = N_IN + N_OUT

            def gate_up(e, need, slot, first=False):
                pe.wait_ge(w_split, need + 1)
                if not first:
                    pe.wait_ge(gate_silu, e)
                project(pair[0], slot % WS).then_inc(w_used, 1)
                pe.wait_ge(w_split, need + 2)
                if not first:
                    pe.wait_ge(ufull_ready, e)
                project(pair[1], (slot + 1) % WS).then_inc(w_used, 1)

            def down(bk, need, slot):
                pe.wait_ge(w_split, need + 2)
                pe.wait_ge(u_ready, bk * 2 + 2)
                for i in range(TT):
                    pe.wait_ge(y_added, bk * TT + max(0, i - 1) + CREDIT)
                    tokens = slice(i * P, (i + 1) * P)
                    for f in range(2):
                        i_ = token_product(pair[2 + i % 2], u_hi[:, f, tokens], u_lo[:, f, tokens],
                                           w_hi[:, (slot + f) % WS, :], w_lo[:, (slot + f) % WS, :], f == 0, f == 1)
                    if i < TT - 1:
                        i_.then_inc(down_ready, 1)
                    else:
                        i_.then_inc(w_used, 2)
            gate_up(0, F0, F0, first=True)
            with pe.Fori(0, FB - 1) as bk:
                gate_up(bk * 2 + 1, bk * 6 + (F0 + 2), F0 + 2)
                gate_up(bk * 2 + 2, bk * 6 + (F0 + 4), F0 + 4)
                down(bk, bk * 6 + (F0 + 6), F0 + 6)
            gate_up(FFT - 1, 6 * (FB - 1) + F0 + 2, F0 + 2)
            pe.wait_ge(ufull_ready, FFT)
            gg_rows(1, pair[0])
            down(FB - 1, 6 * (FB - 1) + F0 + 4, F0 + 4)


_SHAPES = [("x", (1, S, D)), ("c", (1, D)), ("w_ada", (1, D, 6 * D)), ("b_ada", (1, 6 * D)), ("g_pre_mix", (1, D)),
           ("g_post_mix", (1, D)), ("w_in", (1, D, 3 * D)), ("conv_w", (1, TAPS, CT * P)), ("conv_b", (1, CT * P)),
           ("conv_ln_g", (1, CT * P)), ("conv_ln_b", (1, CT * P)), ("hgrn_lower_bounds", (1, HEADS * P)),
           ("hgrn_norm_g", (1, P)), ("w_out", (1, D, D)), ("g_pre_ffn", (1, D)), ("g_post_ffn", (1, D)),
           ("w_ffn_in", (1, D, 2 * D_FF)), ("w_ffn_out", (1, D_FF, D))]


def kernel(**inputs):
    import numpy as np
    import concourse.bacc as bacc
    from concourse.bass_utils import run_bass_kernel_spmd

    nc = bacc.Bacc("TRN2", target_bir_lowering=False, num_devices=1)
    arrays, t_in = {}, {}
    for name, shape in _SHAPES:
        a = np.ascontiguousarray(inputs[name])
        assert a.shape == shape, (name, a.shape)
        arrays[f"in_{name}"] = a
        t_in[name] = nc.dram_tensor(f"in_{name}", a.shape, mybir.dt.from_np(a.dtype), kind="ExternalInput").ap()
    out = nc.dram_tensor("out", (1, S, D), F32, kind="ExternalOutput").ap()
    build(nc, t_in, out)
    result = run_bass_kernel_spmd(nc, [arrays], core_ids=[0])
    return result.results[0]["out"]
```

```python
from contextlib import ExitStack

import concourse.bass as bass
from concourse import mybir

F32 = mybir.dt.float32
F32R = mybir.dt.float32r
BF16 = mybir.dt.bfloat16
I32 = mybir.dt.int32
ALU = mybir.AluOpType
ACT = mybir.ActivationFunctionType
AX_X = mybir.AxisListType.X
ds = bass.ds

P = 128
D = 1024
S = 1024
KT = D // P
TT = S // P
HALF = 512
CHUNK = 64
TAPS = 31
HEADS = 4
CT = 4
FFT = 22
FB = FFT // 2
D_FF = FFT * P
EPS = 1e-6
LEVELS = [64, 32, 16, 8, 4, 2]

RAW = 2
WS = 3
N_IN = 6 * 4
N_OUT = KT
N_FFN = 3 * FFT
N_CHUNKS = N_IN + N_OUT + N_FFN

ROW_C, ROW_GPRE1, ROW_GPOST1, ROW_GPRE2, ROW_GPOST2 = 0, 8, 16, 24, 32
ROW_BADA, ROW_CB, ROW_LNG, ROW_LNB, ROW_LB, ROW_NG, ROWS = 40, 88, 92, 96, 100, 104, 105


POOL_F = ["D0", "D1", "DKD", "D2", "KD", "QE", "D3", "D4", "D5"]
POOL_B = ["LO"]
ACT_F = ["KC", "VC", "EL0", "E0", "EL1", "E1", "EKD", "EB", "EL2", "E2", "EL3", "E3", "EL4", "E4", "EL5", "E5", "KDT"]
ACT_B = ["SQ"] * HEADS + ["LN", "RSTD"]
ACT_H = ["HI"]
DVE_F = ["XL0", "X0", "XL1", "X1", "PD", "XL2", "X2", "P0", "XL3", "X3", "P1", "XL4", "X4", "P2",
         "XL5", "X5", "P3"] + ["ST1"] * 4 + ["ST0"] * 4 + ["P4", "P5"]
DVE_B = ["ON", "MIX"]
PE_F = ["DIAG", "S0", "S1", "S2", "KDT", "S3", "S4", "C0", "C1", "S5"]
PE_B = ["O", "OT"]
VEC_LOADS = 12
CREDIT = 1
LN_DVE = 3 * CT


class Tally:

    def __init__(self, eng, sem):
        self.eng, self.sem, self.base, self.turn, self.per, self.n = eng, sem, 0, 0, 0, 0

    def done(self, instruction):
        instruction.then_inc(self.sem, 1)
        self.n += 1

    def wait(self, behind=0):
        self.eng.wait_ge(self.sem, self.base + self.turn * self.per + self.n - behind)

    def last(self):
        return self.sem, self.base + self.turn * self.per + self.n

    def enter(self, turn, per):
        self.base, self.turn, self.per, self.n = self.base + self.n, turn, per, 0

    def leave(self, turns):
        assert self.n == self.per, (self.n, self.per)
        self.base, self.turn, self.per, self.n = self.base + self.per * turns, 0, 0, 0


def build(nc, t_in, out):
    x_d = t_in["x"].rearrange("a (i p) d -> (a p) i d", p=P)
    out_d = out.rearrange("a (i p) d -> (a p) i d", p=P)
    w_ada_d = t_in["w_ada"].rearrange("l (kt p) n -> (l p) kt n", p=P)
    w_in_d = t_in["w_in"].rearrange("l (kt p) n -> (l p) kt n", p=P)
    w_out_d = t_in["w_out"].rearrange("l (kt p) n -> (l p) kt n", p=P)
    w_up_d = t_in["w_ffn_in"].rearrange("l (kt p) n -> (l p) kt n", p=P)
    w_down_d = t_in["w_ffn_out"].rearrange("l (f p) n -> (l p) f n", p=P)
    y_spill = nc.dram_tensor("conv_spill", [P, CT, S], F32).ap()
    og_spill = nc.dram_tensor("og_spill", [P, HEADS, S], F32).ap()

    ctx = ExitStack()
    with ctx:
        def sem(name):
            return ctx.enter_context(nc.semaphore(name))

        def group(specs):
            made = []
            with ExitStack() as place:
                for name, shape, dt in specs:
                    made.append(place.enter_context(nc.sbuf_tensor(name, shape, dt)))
            return made

        def keep(name, shape, dt=F32):
            return ctx.enter_context(nc.sbuf_tensor(name, shape, dt))

        ident = keep("ident", [P, P])
        ones = keep("ones", [P, P])
        masks = keep("masks", [P, len(LEVELS), P])
        scan_keep = keep("scan_keep", [P, S], BF16)
        rows_a = keep("rows_a", [ROWS, P])
        rows_b = keep("rows_b", [TAPS * CT, P])
        vec = keep("vec", [P, ROWS])
        conv_w_col = keep("conv_w_col", [P, TAPS * CT])
        mod = keep("mod", [P, 48])
        cond = keep("cond", [P, KT])
        gs = keep("gs", [P, 2, KT])
        gg = keep("gg", [P, 2, KT])
        lb_tmp = keep("lb_tmp", [P, 4, HEADS])
        one_less_lb = keep("one_less_lb", [P, HEADS])
        log_one_less_lb = keep("log_one_less_lb", [P, HEADS])
        tile_w = keep("tile_w", [P, TAPS])
        tile_cols = keep("tile_cols", [P, 3])
        ss = keep("ss", [P, 4, TT])
        rs = keep("rs", [P, 4, TT])
        ggb = keep("ggb", [P, D])
        ekd = keep("ekd", [P, HEADS, P])
        raw = keep("raw", [P, RAW, D])
        w_hi = keep("w_hi", [P, WS, D], F32R)
        w_lo = keep("w_lo", [P, WS, D], F32R)

        w2k = [P, HEADS, P]
        xr, dd, ee, qe, kd, kc, kdt, vc = group([
            ("xr", [P, 3, HEADS, P], F32), ("dd", [P, 3, HEADS, P], F32), ("ee", [P, 3, HEADS, P], F32),
            ("qe", [P, 2, HEADS, P], F32), ("kd", w2k, F32), ("kc", w2k, F32), ("kdt", w2k, F32),
            ("vc", [P, 2, HEADS, P], F32)])
        ada0, = group([("ada0", [P, KT, 2 * D], F32)])
        ha_hi = keep("ha_hi", [P, 4, S], F32R)
        ha_lo = keep("ha_lo", [P, 4, S], F32R)
        hb_hi = keep("hb_hi", [P, 4, S], F32R)
        hb_lo = keep("hb_lo", [P, 4, S], F32R)

        x0, acc0, full0 = group([("x0", [P, TT, D], F32), ("acc0", [P, 2 * D], F32), ("full0", [P, 2, HALF], F32)])
        q, k, b, v, ada, acc, ogt, vt, sg, u, y = group([
            ("q", [P, HEADS, S], F32), ("k", [P, HEADS, S], F32), ("b", [P, HEADS, S], F32),
            ("v", [P, TT, HEADS * P], F32), ("ada", [P, 2, D], F32), ("acc", [P, D], F32),
            ("ogt", [P, S], F32), ("vt", [P, S], F32), ("sg", [P, S], F32),
            ("u", [P, S + TAPS - 1], F32), ("y", [P, S], F32)])
        _, pmat, state, ogc, mixf, eb, sq, on = group([
            ("qkbv", [P, 4 * HEADS * S], F32), ("pmat", [P, 2, HEADS, P], F32), ("state", [P, 4, HEADS, P], F32),
            ("ogc", [P, 2, HEADS, P], F32), ("mixf", w2k, F32), ("eb", w2k, F32), ("sq", w2k, F32), ("on", w2k, F32)])
        wo_hi, wo_lo, x1, xs, tail_tmp = group([
            ("wo_hi", [P, N_OUT - WS, D], F32R), ("wo_lo", [P, N_OUT - WS, D], F32R), ("x1", [P, TT, D], F32),
            ("xs", [P, 4, D], F32), ("tail_tmp", [P, 2, D], F32)])
        _, y4, ln_sq, ln_rs, ln_f = group([
            ("wo_", [P, 2 * (N_OUT - WS), D], F32), ("y4", [P, CT, S], F32), ("ln_sq", [P, 2, S], F32),
            ("ln_rs", [P, S], F32), ("ln_f", [P, 2, S], F32)])
        _, full1 = group([("before_full1", [P, 2 * (N_OUT - WS) + TT + 4, D], F32), ("full1", [P, 2, HALF], F32)])
        yt, gate, ufull, _, u_hi, u_lo = group([
            ("yt", [P, TT, D], F32), ("gate", [P, S], F32), ("ufull", [P, S], F32), ("x1_", [P, TT, D], F32),
            ("u_hi", [P, 2, S], F32R), ("u_lo", [P, 2, S], F32R)])
        pair = [ctx.enter_context(nc.psum_tensor(f"pair{i}", [P, S], F32)) for i in range(4)]

        def bank(i):
            return pair[i // 2][:, (i % 2) * HALF:(i % 2 + 1) * HALF]

        consts_ready = sem("consts_ready")
        vec_loaded = sem("vec_loaded")
        vec_turned = sem("vec_turned")
        vec_ready = sem("vec_ready")
        cond_ready = sem("cond_ready")
        x_loaded = [sem(f"x_loaded{i}") for i in range(4)]
        x1_loaded = [sem(f"x1_loaded{i}") for i in range(4)]
        ada0_loaded = [sem(f"ada0_loaded{i}") for i in range(KT)]
        ada0_used = sem("ada0_used")
        mod0_summed = sem("mod0_summed")
        mod_ready = sem("mod_ready")
        ss_ready = sem("ss_ready")
        xs_ready = sem("xs_ready")
        turned = sem("turned")
        full_ready = sem("full_ready")
        full_act = sem("full_act")
        hi_ready = sem("hi_ready")
        h_ready = sem("h_ready")
        raw_loaded = [sem(f"raw_loaded{i}") for i in range(RAW)]
        w_split = sem("w_split")
        w_used = sem("w_used")
        gate_sig = sem("gate_sig")
        q_evac = sem("q_evac")
        og_evac = sem("og_evac")
        vt_evac = sem("vt_evac")
        z_evac = sem("z_evac")
        u_evac = sem("u_evac")
        ada_loaded = [sem(f"ada_loaded{i}") for i in range(2)]
        ada_used = sem("ada_used")
        modt_summed = sem("modt_summed")
        modt_ready = sem("modt_ready")
        ring_free = sem("ring_free")
        z_log = sem("z_log")
        tap_done = sem("tap_done")
        y_stored = sem("y_stored")
        og_stored = sem("og_stored")
        v_turned = sem("v_turned")
        v_ready = sem("v_ready")
        act_self = sem("act_self")
        dve_self = sem("dve_self")
        pool_self = sem("pool_self")
        at_pool_f, at_pool_b = sem("at_pool_f"), sem("at_pool_b")
        at_act_f, at_act_b, at_act_h = sem("at_act_f"), sem("at_act_b"), sem("at_act_h")
        at_dve_f, at_dve_b = sem("at_dve_f"), sem("at_dve_b")
        at_pe_f, at_pe_b = sem("at_pe_f"), sem("at_pe_b")
        at_clear = sem("at_clear")
        b_ready = sem("b_ready")
        ogc_loaded = [sem(f"ogc_loaded{i}") for i in range(2)]
        y4_loaded = sem("y4_loaded")
        ln_added = sem("ln_added")
        ln_pe = sem("ln_pe")
        ln_dve = sem("ln_dve")
        ln_act = sem("ln_act")
        ggb_pe = sem("ggb_pe")
        ggb_ready = sem("ggb_ready")
        tail_ss = sem("tail_ss")
        tail_read = sem("tail_read")
        tail_done = sem("tail_done")
        last_done = sem("last_done")
        x1_ss = sem("x1_ss")
        gate_silu = sem("gate_silu")
        ufull_ready = sem("ufull_ready")
        uhi_ready = sem("uhi_ready")
        u_ready = sem("u_ready")
        down_ready = sem("down_ready")
        y_added = sem("y_added")
        yt_zero = sem("yt_zero")
        out_stored = sem("out_stored")

        def after(order, turn, name):
            return turn * len(order) + (len(order) - order[::-1].index(name))

        lists = {at_pool_f: POOL_F, at_pool_b: POOL_B, at_act_f: ACT_F, at_act_b: ACT_B, at_act_h: ACT_H,
                 at_dve_f: DVE_F, at_dve_b: DVE_B, at_pe_f: PE_F, at_pe_b: PE_B}

        def event(s_, turn, name):
            return s_, after(lists[s_], turn, name)

        class Signals:

            def __init__(self, s_):
                self.s_, self.given = s_, []

            def __call__(self, name, i_):
                i_.then_inc(self.s_, 1)
                self.given.append(name)

            def close(self):
                assert self.given == lists[self.s_], self.given

        def attention_steps(eng, step):
            step(0, None, 0)
            step(1, 0, 1)
            with eng.Fori(2, TT - 1, 2) as i:
                step(i, i + (-1), 0)
                step(i + 1, i, 1)
            step(None, TT - 1, 0)

        OUT_K = [4, 5, 6, 7, 0, 1, 2, 3]

        def turn_group(g):
            return g % KT, g // KT

        def out_pair(i):
            return pair[i + 2 if i < 2 else i % 2]

        def modulated(call, g):
            return full_act if g % 2 else full_ready, 8 * call + g // 2 + 1

        def score_bank(n):
            return bank((0, 1, 6, 7)[(n + 1) % 4])

        def ogc_count(turn, par):
            return 8 * (turn + (2 - par))

        passed = sem("passed")

        def apart(eng, *waits):
            for s_, n in waits:
                eng.wait_ge(s_, n)
            eng.sem_inc(passed, 1)

        block = ctx.enter_context(nc.Block())

        @block.sync
        def _(sp):
            a = lambda t, n: t.rearrange("l (r c) -> (l r) c", c=P)
            for row, name, n in ((ROW_C, "c", 8), (ROW_GPRE1, "g_pre_mix", 8), (ROW_GPOST1, "g_post_mix", 8),
                                 (ROW_GPRE2, "g_pre_ffn", 8), (ROW_GPOST2, "g_post_ffn", 8),
                                 (ROW_BADA, "b_ada", 48), (ROW_CB, "conv_b", 4), (ROW_LNG, "conv_ln_g", 4),
                                 (ROW_LNB, "conv_ln_b", 4), (ROW_LB, "hgrn_lower_bounds", 4),
                                 (ROW_NG, "hgrn_norm_g", 1)):
                sp.dma_start(rows_a[row:row + n, :], a(t_in[name], n)).then_inc(vec_loaded, 16)
            sp.dma_start(rows_b[:, :], t_in["conv_w"].rearrange("l j (t c) -> (l j t) c", c=P)).then_inc(vec_loaded, 16)
            for kt in range(2, KT):
                sp.dma_start(ada0[:, kt, :], w_ada_d[:, kt, 0:2 * D]).then_inc(ada0_loaded[kt], 16)
            for i in range(4):
                sp.dma_start(x0[:, 2 * i:2 * i + 2, :], x_d[:, 2 * i:2 * i + 2, :]).then_inc(x_loaded[i], 16)

            def load(g, src, ready):
                if ready is not None:
                    apart(sp, (w_split, ready))
                sp.dma_start(raw[:, g % RAW, :] if src.shape[1] != KT else
                             raw[:, g % RAW, :].rearrange("p (kt c) -> p kt c", kt=KT), src
                             ).then_inc(raw_loaded[g % RAW], 16)

            def in_tile(base, t):
                return w_in_d[:, :, ds(t * P + base * P, P)]

            def in_round(t, first):
                for j, base in enumerate((4, 0, 12, 8, 20, 16)):
                    load(j, in_tile(base, t), None if first and j < RAW else t * 6 + (j - 1))
                    if j == 2 and not first:
                        store_conv(t + (-1))

            def store_conv(t):
                apart(sp, (tap_done, t * 2 * TAPS + 2 * TAPS + CREDIT))
                sp.dma_start(y_spill[:, ds(t, 1), :], y[:, :].unsqueeze(1)).then_inc(y_stored, 16)
            in_round(0, True)
            with sp.Fori(1, CT) as t:
                in_round(t, False)
            ahead = RAW + WS
            for n in range(ahead):
                if n == WS:
                    store_conv(CT - 1)
                load(N_IN + n, w_out_d[:, OUT_K[n]:OUT_K[n] + 1, :], N_IN + n - 1)
            sp.wait_ge(og_stored, 16 * HEADS + 16 * CREDIT)
            sp.wait_ge(v_ready, HEADS + CREDIT)
            for par in range(2):
                sp.dma_start(ogc[:, par], og_spill[:, :, par * P:(par + 1) * P]).then_inc(ogc_loaded[par], 16)
            with sp.Fori(2, TT - 1, 2) as c:
                for par in range(2):
                    apart(sp, event(at_dve_b, c + (par - 2), "MIX"))
                    sp.dma_start(ogc[:, par], og_spill[:, :, ds(c * P + par * P, P)]).then_inc(ogc_loaded[par], 16)
            sp.wait_ge(*event(at_dve_f, TT - 1, "P5"))
            sp.wait_ge(y_stored, 16 * CT + 16 * CREDIT)
            sp.dma_start(y4[:, :, :], y_spill).then_inc(y4_loaded, 16)
            for n in range(ahead, N_OUT):
                load(N_IN + n, w_out_d[:, OUT_K[n]:OUT_K[n] + 1, :], N_IN + n - 1)
            for i, (s_, n) in enumerate([(ln_act, CT + 1 + 3), (ln_act, CT + 1 + 7), (ln_dve, LN_DVE), (ln_dve, LN_DVE)]):
                sp.wait_ge(s_, n)
                sp.dma_start(x1[:, 2 * i:2 * i + 2, :], x_d[:, 2 * i:2 * i + 2, :]).then_inc(x1_loaded[i], 16)

            G0 = N_IN + N_OUT
            load(G0, w_up_d[:, :, 0:P], G0 - 1)
            load(G0 + 1, w_up_d[:, :, D_FF:D_FF + P], G0)

            def ffn_round(bk, last):
                g = G0 + 2
                srcs = [w_up_d[:, :, ds(bk * 2 * P + P, P)], w_up_d[:, :, ds(bk * 2 * P + P + D_FF, P)]]
                if not last:
                    srcs += [w_up_d[:, :, ds(bk * 2 * P + 2 * P, P)], w_up_d[:, :, ds(bk * 2 * P + 2 * P + D_FF, P)]]
                srcs += [w_down_d[:, ds(bk * 2, 1), :], w_down_d[:, ds(bk * 2 + 1, 1), :]]
                for j, src in enumerate(srcs):
                    load(g + j, src, bk * 6 + (g + j - 1))
            with sp.Fori(0, FB - 1) as bk:
                ffn_round(bk, False)
            ffn_round(FB - 1, True)
            for i in range(TT):
                if i < TT - 1:
                    sp.wait_ge(tail_done, TT + i + 1)
                else:
                    sp.wait_ge(last_done, 1)
                sp.dma_start(out_d[:, i, :], x1[:, i, :]).then_inc(out_stored, 16)
            sp.wait_ge(out_stored, 16 * TT)

        @block.gpsimd
        def _(pool):
            me = Tally(pool, pool_self)
            me.done(pool.memset(ident[:, :], 0.0))
            pool.memset(ones[:, :], 1.0).then_inc(consts_ready, 1)
            me.done(pool.memset(masks[:, :, :], 1.0))
            me.wait()
            pool.affine_select(out=ident[:, :], in_=ident[:, :], compare_op=ALU.not_equal, fill=1.0, base=0,
                               pattern=[[-1, P]], channel_multiplier=1).then_inc(consts_ready, 1)
            for n, size in enumerate(LEVELS):
                half, blocks = size // 2, P // size
                m = masks[:, n, :].rearrange("s (b h c) -> s b h c", h=2, c=half)
                me.done(pool.memset(m[:, :, 0, :], 0.0))
                right = m[:, :, 1, :]
                me.done(pool.affine_select(out=right, in_=right, compare_op=ALU.is_ge, fill=0.0, base=0,
                                           pattern=[[-size, blocks], [0, half]], channel_multiplier=1))
                me.wait()
                me.done(pool.affine_select(out=right, in_=right, compare_op=ALU.is_ge, fill=0.0, base=half - 1,
                                           pattern=[[size, blocks], [0, half]], channel_multiplier=-1))
            me.wait()
            pool.sem_inc(consts_ready, 1)

            def split(j, loads, free, to=None, after_ring=False):
                apart(pool, (raw_loaded[j % RAW], loads), *([(w_used, free)] if free is not None else []),
                      *([(ring_free, 1)] if after_ring else []))
                hi, lo = to if to is not None else (w_hi[:, j % WS, :], w_lo[:, j % WS, :])
                src = raw[:, j % RAW, :]
                me.done(pool.tensor_copy(hi, src))
                me.wait()
                pool.tensor_tensor(lo, src, hi, ALU.subtract).then_inc(w_split, 1)

            for j in range(6):
                split(j, 16 * (j // RAW + 1), None if j < WS else j - WS + 1)
            def split_rounds(first, turns):
                r0 = first // 6
                with pool.Fori(r0, r0 + turns) as r:
                    me.enter(r + (-r0), 6)
                    for j in range(6):
                        split(j, r * 16 * (6 // RAW) + 16 * (j // RAW + 1), r * 6 + (j - WS + 1))
                me.leave(turns)

            def split_some(first, last):
                for g in range(first, last):
                    split(g % 6, 16 * (g // RAW + 1), g - WS + 1)
            split_rounds(6, 3)
            split_some(N_IN, N_IN + WS)

            def split_apart(n):
                g = N_IN + n
                split(g, 16 * (g // RAW + 1), None, (wo_hi[:, n - WS, :], wo_lo[:, n - WS, :]))

            pool.wait_ge(modt_summed, HEADS)
            me.done(pool.memset(pmat[:, :, :, :], 0.0))
            me.wait()
            pool.memset(state[:, 0, :, :], 0.0).then_inc(at_clear, 1)
            pool.wait_ge(b_ready, HEADS)
            pool.wait_ge(w_used, N_IN)

            def step(i, back, par):
                if i is not None:
                    signal = Signals(at_pool_f)
                    cols = ds(i * P, P)
                    first = isinstance(i, int) and i == 0
                    bch = b[:, :, cols].rearrange("p h (g c) -> p h g c", c=CHUNK)

                    def diff(n):
                        if n >= 2:
                            apart(pool, event(at_act_f, i, f"E{n - 3}" if n > 2 else "EKD"))
                        elif n < 2 and not first:
                            apart(pool, event(at_act_f, i - 1, f"E{n + 3}"))
                        size = LEVELS[n]
                        bv = b[:, :, cols].rearrange("p h (g c) -> p h g c", c=size)
                        ref = bv[:, :, :, size // 2 - 1:size // 2].to_broadcast([P, HEADS, P // size, size])
                        signal(f"D{n}", pool.tensor_tensor(dd[:, n % 3].rearrange("p h (g c) -> p h g c", c=size),
                                                           bv, ref, ALU.subtract))
                    diff(0)
                    diff(1)
                    if not first:
                        apart(pool, event(at_act_f, i - 1, "E5"))
                    signal("DKD", pool.tensor_tensor(dd[:, 2].rearrange("p h (g c) -> p h g c", c=CHUNK), bch,
                                                     bch[:, :, :, CHUNK - 1:CHUNK].to_broadcast([P, HEADS, 2, CHUNK]),
                                                     ALU.subtract))
                    diff(2)
                    if not first:
                        apart(pool, event(at_pe_f, i - 1, "KDT"))
                    signal("KD", pool.tensor_tensor(kd[:, :, :], k[:, :, cols], ekd[:, :, :], ALU.mult))
                    apart(pool, event(at_act_f, i, "EB"))
                    signal("QE", pool.tensor_tensor(qe[:, par], q[:, :, cols], eb[:, :, :], ALU.mult))
                    diff(3)
                    low_before(back)
                    for n in range(4, 6):
                        diff(n)
                    signal.close()
                else:
                    low_before(back)
                    pool.wait_ge(*event(at_dve_f, back, "P5"))
                    split_apart(WS)
                    low(back)

            def low_before(back):
                if back is not None and not (isinstance(back, int) and back == 0):
                    low(back - 1)

            def low(back):
                signal = Signals(at_pool_b)
                apart(pool, event(at_act_h, back, "HI"))
                signal("LO", pool.tensor_tensor(hb_lo[:, :, ds(back * P, P)], mixf[:, :, :],
                                                hb_hi[:, :, ds(back * P, P)], ALU.subtract))
                signal.close()
            attention_steps(pool, step)

            for n in range(WS + 1, N_OUT):
                split_apart(n)
            G0 = N_IN + N_OUT
            for g in range(G0, G0 + WS):
                split(g % 6, 16 * (g // RAW + 1), None, after_ring=True)
            pool.wait_ge(w_used, G0)
            pool.memset(yt[:, :, :], 0.0).then_inc(yt_zero, 1)
            first = -(-(G0 + WS) // 6) * 6
            split_some(G0 + WS, first)
            split_rounds(first, (N_CHUNKS - first) // 6)
            split_some(N_CHUNKS - N_CHUNKS % 6, N_CHUNKS)
            for i in range(TT - 1):
                pool.wait_ge(tail_read, TT + i + 1)
                pool.tensor_tensor(x1[:, i, :], x1[:, i, :], tail_tmp[:, i % 2, :], ALU.add).then_inc(tail_done, 1)

        @block.scalar
        def _(act):
            me = Tally(act, act_self)
            for s_ in (og_evac, vt_evac, v_ready):
                act.sem_inc(s_, CREDIT)
            for s_ in (og_stored, y_stored):
                act.sem_inc(s_, 16 * CREDIT)

            def root_mean_square(src, junk, col, which, count):
                me.done(act.activation(junk, src, ACT.Square, accum_out=ss[:, which, col:col + 1]))
                me.wait()
                return act.activation(rs[:, which, col:col + 1], ss[:, which, col:col + 1], ACT.Sqrt,
                                      scale=1.0 / count, bias=EPS)

            for kt in range(2):
                act.dma_start(ada0[:, kt, :], w_ada_d[:, kt, 0:2 * D]).then_inc(ada0_loaded[kt], 16)
            act.wait_ge(vec_ready, 2)
            act.activation(cond[:, :], vec[:, ROW_C:ROW_C + KT], ACT.Silu).then_inc(cond_ready, 1)
            act.activation(lb_tmp[:, 1, :], lb_tmp[:, 0, :], ACT.Exp).then_inc(cond_ready, 1)
            act.wait_ge(vec_ready, 3)
            act.activation(log_one_less_lb[:, :], one_less_lb[:, :], ACT.Ln).then_inc(cond_ready, 1)

            def hi_parts(call, full, groups):
                for g in groups:
                    kt, half = turn_group(g)
                    if g % 2:
                        act.wait_ge(turned, 16 * call + g + 1)
                        if g > 1:
                            act.wait_ge(h_ready, 16 * call + g - 1)
                        act.activation(full[:, 1, :], bank(4 * call + g % 4), ACT.Identity, scale=gs[:, call, kt:kt + 1],
                                       bias=mod[:, 24 * call + kt:24 * call + kt + 1]).then_inc(full_act, 1)
                    act.wait_ge(*modulated(call, g))
                    dst = (ha_hi if kt < 4 else hb_hi)[:, kt % 4, half * HALF:(half + 1) * HALF]
                    act.activation(dst, full[:, g % 2, :], ACT.Copy).then_inc(hi_ready, 1)
            for i in range(TT):
                act.wait_ge(x_loaded[i // 2], 16)
                root_mean_square(x0[:, i, :], pair[2][:, :], i, 0, D).then_inc(ss_ready, 1)
            hi_parts(0, full0, range(16))

            act.wait_ge(h_ready, 16)
            with act.Fori(0, 4) as t:
                me.enter(t, 3)

                def ada_loads(js):
                    for j in js:
                        act.wait_ge(ada_used, t * KT + max(0, j - 1) + CREDIT)
                        act.dma_start(ada[:, j % 2, :], w_ada_d[:, j, ds(t * D + 2 * D, D)]
                                      ).then_inc(ada_loaded[j % 2], 16)
                ada_loads(range(5))
                act.wait_ge(w_used, t * 6 + 1)
                act.wait_ge(u_evac, t + CREDIT)
                act.activation(sg[:, :], pair[0][:, :], ACT.Sigmoid).then_inc(gate_sig, 1)
                ada_loads(range(5, KT))
                apart(act, (w_used, t * 6 + 3))
                me.done(act.activation(k[:, t, :], pair[0][:, :], ACT.Sigmoid, scale=-1.0))
                me.done(act.activation(b[:, t, :], pair[0][:, :], ACT.Abs))
                apart(act, me.last())
                me.done(act.activation(b[:, t, :], b[:, t, :], ACT.Exp, scale=-1.0))
                apart(act, me.last())
                act.activation(b[:, t, :], b[:, t, :], ACT.Ln, bias=1.0).then_inc(z_log, 1)
                apart(act, (w_used, t * 6 + 4))
                act.activation(q[:, t, :], pair[1][:, :], ACT.Silu).then_inc(q_evac, 1)
                act.wait_ge(w_used, t * 6 + 5)
                act.wait_ge(og_stored, t * 16 + 16 * CREDIT)
                act.activation(ogt[:, :], pair[0][:, :], ACT.Silu).then_inc(og_evac, 1)
                act.wait_ge(og_evac, t + 1 + CREDIT)
                act.dma_start(og_spill[:, t, :], ogt[:, :]).then_inc(og_stored, 16)
                act.wait_ge(w_used, t * 6 + 6)
                act.activation(vt[:, :], pair[1][:, :], ACT.Copy).then_inc(vt_evac, 1)
                apart(act, (v_turned, t + 1))
                act.activation(v[:, :, ds(t * P, P)], pair[2][:, :].rearrange("s (c n) -> s c n", n=P),
                               ACT.Copy).then_inc(v_ready, 1)
            me.leave(4)

            act.wait_ge(b_ready, HEADS)
            act.wait_ge(v_ready, HEADS + CREDIT)

            act.preload_act_table_set("natural_log_exp_and_others")

            def step(i, back, par):
                if i is not None:
                    first = isinstance(i, int) and i == 0
                    signal = Signals(at_act_f)
                    cols = ds(i * P, P)
                    if not first:
                        apart(act, event(at_pe_f, i - 1, "DIAG"))
                    signal("KC", act.activation(kc[:, :, :], k[:, :, cols], ACT.Copy))
                    signal("VC", act.activation(vc[:, par], v[:, i, :].rearrange("s (h n) -> s h n", n=P), ACT.Copy))

                    def decay(n):
                        act.wait_ge(*event(at_pool_f, i, f"D{n}"))
                        if n >= 3:
                            act.wait_ge(*event(at_dve_f, i, f"X{n - 3}"))
                        elif not first:
                            act.wait_ge(*event(at_dve_f, i - 1, f"X{n + 3}"))
                        dv, ev = (w[:, n % 3].rearrange("p h (g s c) -> p (h g) s c", s=2, c=LEVELS[n] // 2)
                                  for w in (dd, ee))
                        signal(f"EL{n}", act.activation(ev[:, :, 0, :], dv[:, :, 0, :], ACT.Exp, scale=-1.0))
                        signal(f"E{n}", act.activation(ev[:, :, 1, :], dv[:, :, 1, :], ACT.Exp))
                    decay(0)
                    decay(1)
                    act.wait_ge(*event(at_pool_f, i, "DKD"))
                    if not first:
                        act.wait_ge(*event(at_pool_f, i - 1, "KD"))
                    signal("EKD", act.activation(ekd[:, :, :], dd[:, 2], ACT.Exp, scale=-1.0))
                    if not first:
                        apart(act, event(at_dve_f, i - 1, "ST0"), event(at_pool_f, i - 1, "QE"))
                    signal("EB", act.activation(eb[:, :, :], b[:, :, cols], ACT.Exp))
                if back is not None and not (isinstance(back, int) and back == 0):
                    high(back - 1)
                if i is not None:
                    for n in range(2, 6):
                        decay(n)
                    act.wait_ge(*event(at_pe_f, i, "KDT"))
                    signal("KDT", act.activation(kdt[:, :, :], bank(2).rearrange("s (h n) -> s h n", n=P), ACT.Copy))
                    signal.close()
                if back is not None:
                    signal_b = Signals(at_act_b)
                    act.wait_ge(*event(at_pe_b, back, "O"))
                    for h in range(HEADS):
                        signal_b("SQ", act.activation(sq[:, h, :], bank(5)[:, h * P:(h + 1) * P], ACT.Square,
                                                      accum_out=ss[:, 2, h:h + 1]))
                if back is not None:
                    act.wait_ge(*event(at_act_b, back, "SQ"))
                    signal_b("LN", act.activation(rs[:, 2, 0:4], ss[:, 2, 0:4], ACT.Ln, scale=1.0 / P, bias=EPS))
                    act.wait_ge(*event(at_act_b, back, "LN"))
                    signal_b("RSTD", act.activation(rs[:, 2, 4:8], rs[:, 2, 0:4], ACT.Exp, scale=-0.5))
                    signal_b.close()
                if i is None:
                    high(back)

            def high(back):
                signal_h = Signals(at_act_h)
                apart(act, event(at_dve_b, back, "MIX"))
                signal_h("HI", act.activation(hb_hi[:, :, ds(back * P, P)], mixf[:, :, :], ACT.Copy))
                signal_h.close()
            attention_steps(act, step)

            for t in range(CT):
                act.wait_ge(ln_dve, t + 1)
                if t >= 2:
                    act.wait_ge(ln_added, CT)
                act.activation(ln_sq[:, t % 2, :], y4[:, t, :], ACT.Square).then_inc(ln_act, 1)
            act.wait_ge(ln_pe, 2)
            me.done(act.activation(ln_rs[:, :], pair[1][:, :], ACT.Ln, scale=1.0 / (CT * P), bias=EPS))
            me.wait()
            act.activation(ln_rs[:, :], ln_rs[:, :], ACT.Exp, scale=-0.5).then_inc(ln_act, 1)
            for t in range(CT):
                act.wait_ge(ln_dve, CT + t + 1 + max(0, t - 1))
                act.activation(ln_f[:, t % 2, :], y4[:, t, :], ACT.Silu, scale=vec[:, ROW_LNG + t:ROW_LNG + t + 1],
                               bias=vec[:, ROW_LNB + t:ROW_LNB + t + 1]).then_inc(ln_act, 1)
                act.wait_ge(ln_act, CT + 1 + 2 * t + 1)
                act.activation(ha_hi[:, t, :], ln_f[:, t % 2, :], ACT.Copy).then_inc(ln_act, 1)

            def tail_norm(src, slot, i):
                root_mean_square(src, tail_tmp[:, slot, :], i, 1, D).then_inc(tail_ss, 1)

            def x1_norm(i):
                act.wait_ge(tail_done, i + 1)
                root_mean_square(x1[:, i, :], tail_tmp[:, 1, :], i, 3, D).then_inc(x1_ss, 1)
            for i in range(TT):
                act.wait_ge(w_used, N_IN + i + 1)
                tail_norm(out_pair(i)[:, :], 1, i)
                x1_norm(i)
                if i in (4, 5):
                    hi_parts(1, full1, range(4 * (i - 4), 4 * (i - 3)))
            hi_parts(1, full1, range(8, 16))

            F0 = N_IN + N_OUT

            def silu_gate(e, used, first=False):
                act.wait_ge(w_used, used)
                if not first:
                    act.wait_ge(ufull_ready, e)
                act.activation(gate[:, :], pair[0][:, :], ACT.Silu).then_inc(gate_silu, 1)

            def u_hi_part(e, slot):
                act.wait_ge(ufull_ready, e + 1)
                act.activation(u_hi[:, slot, :], ufull[:, :], ACT.Copy).then_inc(uhi_ready, 1)
            act.wait_ge(h_ready, 32)
            silu_gate(0, F0 + 1, first=True)
            u_hi_part(0, 0)
            with act.Fori(0, FB - 1) as bk:
                silu_gate(bk * 2 + 1, bk * 6 + (F0 + 3))
                u_hi_part(bk * 2 + 1, 1)
                silu_gate(bk * 2 + 2, bk * 6 + (F0 + 5))
                act.wait_ge(w_used, bk * 6 + (F0 + 8))
                u_hi_part(bk * 2 + 2, 0)
            silu_gate(FFT - 1, 6 * (FB - 1) + F0 + 3)
            u_hi_part(FFT - 1, 1)
            for i in range(TT):
                act.wait_ge(y_added, (FB - 1) * TT + i + 1 + CREDIT)
                if i >= 2:
                    act.wait_ge(tail_done, TT + i - 1)
                tail_norm(yt[:, i, :], i % 2, i)

        @block.vector
        def _(dve):
            me = Tally(dve, dve_self)
            for s_ in (tap_done, ada_used, modt_ready, y_added, u_evac):
                dve.sem_inc(s_, CREDIT)
            me.done(dve.memset(scan_keep[:, :], 1.0))
            me.wait()
            me.done(dve.memset(scan_keep[:, 0:S:CHUNK], 0.0))
            dve.wait_ge(vec_turned, 1)
            dve.tensor_copy(vec[:, :], pair[3][:, 0:ROWS]).then_inc(vec_ready, 1)
            me.done(dve.tensor_copy(conv_w_col[:, :], pair[3][:, P:P + TAPS * CT]))
            dve.wait_ge(vec_ready, 1)
            lbv = vec[:, ROW_LB:ROW_LB + HEADS]
            dve.tensor_tensor(lb_tmp[:, 0, :], lbv, lbv, ALU.subtract).then_inc(vec_ready, 1)
            dve.wait_ge(cond_ready, 2)
            me.done(dve.reciprocal(lb_tmp[:, 2, :], lb_tmp[:, 1, :]))
            me.wait()
            me.done(dve.tensor_tensor(lb_tmp[:, 3, :], lb_tmp[:, 1, :], lb_tmp[:, 2, :], ALU.mult))
            me.wait()
            me.done(dve.tensor_tensor(lb_tmp[:, 2, :], lb_tmp[:, 3, :], lb_tmp[:, 3, :], ALU.subtract))
            me.wait()
            dve.tensor_scalar(one_less_lb[:, :], lb_tmp[:, 2, :], -1.0, 1.0, ALU.mult, ALU.add).then_inc(vec_ready, 1)

            def normalise(dst, src, col, which):
                me.done(dve.reciprocal(rs[:, which, col:col + 1], rs[:, which, col:col + 1]))
                me.wait()
                return dve.tensor_scalar(dst, src, rs[:, which, col:col + 1], None, ALU.mult)

            for kt in range(KT):
                dve.wait_ge(ada0_loaded[kt], 16)
                if kt == 0:
                    dve.wait_ge(cond_ready, 1)
                    i_ = dve.tensor_scalar(acc0[:, :], ada0[:, 0, :], cond[:, 0:1], None, ALU.mult)
                else:
                    dve.wait_ge(ada0_used, kt)
                    i_ = dve.scalar_tensor_tensor(out=acc0[:, :], in0=ada0[:, kt, :], scalar=cond[:, kt:kt + 1],
                                                  in1=acc0[:, :], op0=ALU.mult, op1=ALU.add)
                i_.then_inc(ada0_used, 1)
            for i in range(TT):
                dve.wait_ge(ss_ready, i + 1)
                normalise(x0[:, i, :], x0[:, i, :], i, 0).then_inc(xs_ready, 1)
            dve.wait_ge(mod0_summed, 1)
            me.done(dve.tensor_tensor(mod[:, 0:16], pair[3][:, 256:272], vec[:, ROW_BADA:ROW_BADA + 16], ALU.add))
            me.wait()
            dve.scalar_tensor_tensor(out=gs[:, 0, :], in0=mod[:, 8:16], scalar=1.0,
                                     in1=vec[:, ROW_GPRE1:ROW_GPRE1 + KT], op0=ALU.add, op1=ALU.mult).then_inc(mod_ready, 1)
            dve.wait_ge(mod_ready, 1)

            def modulate(call, full, groups):
                def lo(g):
                    kt, half = turn_group(g)
                    dve.wait_ge(hi_ready, 16 * call + g + 1)
                    cols = slice(half * HALF, (half + 1) * HALF)
                    hi = (ha_hi if kt < 4 else hb_hi)[:, kt % 4, cols]
                    dve.tensor_tensor((ha_lo if kt < 4 else hb_lo)[:, kt % 4, cols], full[:, g % 2, :], hi,
                                      ALU.subtract).then_inc(h_ready, 1)
                for g in groups:
                    kt, half = turn_group(g)
                    if g % 2 == 0:
                        dve.wait_ge(turned, 16 * call + g + 1)
                        if g >= 2:
                            dve.wait_ge(h_ready, 16 * call + g - 1)
                        dve.tensor_scalar(full[:, 0, :], bank(4 * call + g % 4), gs[:, call, kt:kt + 1],
                                          mod[:, 24 * call + kt:24 * call + kt + 1], ALU.mult, ALU.add
                                          ).then_inc(full_ready, 1)
                    if g > groups[0]:
                        lo(g - 1)
                lo(groups[-1])
            modulate(0, full0, range(16))

            dve.wait_ge(h_ready, 16)
            me.done(dve.memset(u[:, 0:TAPS - 1], 0.0))
            IN_DVE = 4 + 2
            cwv = conv_w_col[:, :].rearrange("p (j t) -> p j t", t=CT)
            with dve.Fori(0, 4) as t:
                me.enter(t, IN_DVE)
                dve.wait_ge(tap_done, t * 2 * TAPS + CREDIT)
                me.wait()
                me.done(dve.tensor_copy(tile_w[:, :], cwv[:, :, t]))
                me.done(dve.tensor_copy(tile_cols[:, 0:1], vec[:, ds(t + ROW_CB, 1)]))
                me.done(dve.tensor_copy(tile_cols[:, 1:2], one_less_lb[:, ds(t, 1)]))
                me.done(dve.tensor_copy(lb_tmp[:, 0, 0:1], log_one_less_lb[:, ds(t, 1)]))
                for j in range(KT):
                    dve.wait_ge(ada_loaded[j % 2], t * 16 * (KT // 2) + 16 * (j // 2 + 1))
                    if j == 0:
                        i_ = dve.tensor_scalar(acc[:, :], ada[:, 0, :], cond[:, 0:1], None, ALU.mult)
                    else:
                        dve.wait_ge(ada_used, t * KT + j + CREDIT)
                        i_ = dve.scalar_tensor_tensor(out=acc[:, :], in0=ada[:, j % 2, :], scalar=cond[:, j:j + 1],
                                                      in1=acc[:, :], op0=ALU.mult, op1=ALU.add)
                    i_.then_inc(ada_used, 1)
                me.wait()
                dve.wait_ge(gate_sig, t + 1)
                dve.wait_ge(w_used, t * 6 + 2)
                dve.tensor_tensor(u[:, TAPS - 1:], sg[:, :], pair[1][:, :], ALU.mult).then_inc(u_evac, 1)
                dve.wait_ge(u_evac, t + 1 + CREDIT)
                dve.wait_ge(y_stored, t * 16 + 16 * CREDIT)

                def taps(lo, hi):
                    for j in range(lo, hi):
                        for h in range(2):
                            dst = y[:, h * HALF:(h + 1) * HALF]
                            src = u[:, h * HALF + j:h * HALF + j + HALF]
                            if j == 0:
                                i_ = dve.tensor_scalar(dst, src, tile_w[:, 0:1], tile_cols[:, 0:1], ALU.mult, ALU.add)
                            else:
                                dve.wait_ge(tap_done, t * 2 * TAPS + (2 * j + h - 1) + CREDIT)
                                i_ = dve.scalar_tensor_tensor(out=dst, in0=src, scalar=tile_w[:, j:j + 1], in1=dst,
                                                              op0=ALU.mult, op1=ALU.add)
                            i_.then_inc(tap_done, 1)
                taps(0, 8)
                dve.wait_ge(z_log, t + 1)
                dve.scalar_tensor_tensor(out=b[:, t, :], in0=pair[0][:, :], scalar=0.0, in1=b[:, t, :],
                                         op0=ALU.min, op1=ALU.subtract).then_inc(z_evac, 1)
                dve.wait_ge(z_evac, t + 1)
                me.done(dve.tensor_scalar(b[:, t, :], b[:, t, :], lb_tmp[:, 0, 0:1], None, ALU.add))
                me.done(dve.tensor_scalar(k[:, t, :], k[:, t, :], tile_cols[:, 1:2], None, ALU.mult))
                me.wait()
                dve.tensor_tensor_scan(b[:, t, :], scan_keep[:, :], b[:, t, :], 0.0, ALU.mult, ALU.add).then_inc(b_ready, 1)
                taps(8, TAPS)
                dve.wait_ge(modt_summed, t + 1)
                dve.tensor_tensor(mod[:, ds(t * KT + 16, KT)], pair[3][:, 288:288 + KT],
                                  vec[:, ds(t * KT + (ROW_BADA + 16), KT)], ALU.add).then_inc(modt_ready, 1)
            me.leave(4)
            dve.wait_ge(modt_ready, 4 + CREDIT)
            dve.scalar_tensor_tensor(out=gs[:, 1, :], in0=mod[:, 32:40], scalar=1.0,
                                     in1=vec[:, ROW_GPRE2:ROW_GPRE2 + KT], op0=ALU.add, op1=ALU.mult).then_inc(mod_ready, 1)
            dve.tensor_tensor(gg[:, 0, :], mod[:, 16:24], vec[:, ROW_GPOST1:ROW_GPOST1 + KT], ALU.mult).then_inc(mod_ready, 1)
            dve.tensor_tensor(gg[:, 1, :], mod[:, 40:48], vec[:, ROW_GPOST2:ROW_GPOST2 + KT], ALU.mult).then_inc(mod_ready, 1)

            me.wait()
            dve.wait_ge(w_used, N_IN)
            dve.wait_ge(v_ready, HEADS + CREDIT)
            dve.wait_ge(b_ready, HEADS)
            dve.wait_ge(consts_ready, 3)
            dve.wait_ge(at_clear, 1)

            def step(i, back, par):
                def on_front(s_, name):
                    dve.wait_ge(*event(s_, i, name))
                if i is not None:
                    signal = Signals(at_dve_f)
                    cols = ds(i * P, P)
                if back is not None:
                    signal_b = Signals(at_dve_b)

                def scaled(n):
                    if i is None:
                        return
                    on_front(at_act_f, f"E{n}")
                    ev, xv, kv, qv = (w.rearrange("p h (g s c) -> p h g s c", s=2, c=LEVELS[n] // 2)
                                      for w in (ee[:, n % 3], xr[:, n % 3], k[:, :, cols], q[:, :, cols]))
                    signal(f"XL{n}", dve.tensor_tensor(xv[:, :, :, 0, :], kv[:, :, :, 0, :], ev[:, :, :, 0, :], ALU.mult))
                    signal(f"X{n}", dve.tensor_tensor(xv[:, :, :, 1, :], qv[:, :, :, 1, :], ev[:, :, :, 1, :], ALU.mult))

                def place(n):
                    if i is None:
                        return
                    waits = [event(at_pe_f, i, f"S{n}" if n >= 0 else "DIAG")]
                    if n >= 0:
                        waits.append(event(at_dve_f, i, f"P{n - 1}" if n else "PD"))
                    apart(dve, *waits)
                    mask = masks[:, n, :] if n >= 0 else ident[:, :]
                    signal(f"P{n}" if n >= 0 else "PD",
                           dve.copy_predicated(pmat[:, par], mask.bitcast(I32).unsqueeze(1).to_broadcast([P, HEADS, P]),
                                               score_bank(n).rearrange("s (h n) -> s h n", n=P)))

                def next_state(j):
                    if i is None:
                        return
                    on_front(at_pe_f, f"C{j}")
                    if j:
                        on_front(at_dve_f, "ST1")
                    elif not (isinstance(i, int) and i == 0):
                        dve.wait_ge(*event(at_dve_f, i - 1, "ST0"))
                    last = CHUNK * (j + 1) - 1
                    for h in range(HEADS):
                        signal("ST0" if j else "ST1", dve.scalar_tensor_tensor(
                            out=state[:, (2 * par + j + 1) % 4, h, :], in0=state[:, 2 * par + j, h, :],
                            scalar=eb[:, h, last:last + 1], in1=bank(3 + j)[:, h * P:(h + 1) * P],
                            op0=ALU.mult, op1=ALU.add))
                scaled(0)
                scaled(1)
                place(-1)
                scaled(2)
                place(0)
                scaled(3)
                place(1)
                scaled(4)
                place(2)
                scaled(5)
                place(3)
                next_state(0)
                next_state(1)
                if back is not None:
                    dve.wait_ge(*event(at_act_b, back, "RSTD"))
                    signal_b("ON", dve.tensor_tensor(on[:, :, :], bank(5).rearrange("s (h n) -> s h n", n=P),
                                                     rs[:, 2, 4:8].unsqueeze(2).to_broadcast([P, HEADS, P]), ALU.mult))
                place(4)
                place(5)
                if back is not None:
                    dve.wait_ge(*event(at_pe_b, back, "OT"))
                    dve.wait_ge(ogc_loaded[1 - par], ogc_count(back, 1 - par))
                    if not (isinstance(back, int) and back == 0):
                        dve.wait_ge(*event(at_pool_b, back - 1, "LO"))
                    signal_b("MIX", dve.scalar_tensor_tensor(
                        out=mixf[:, :, :], in0=bank(2).rearrange("p (h n) -> p h n", n=P),
                        scalar=vec[:, ROW_NG:ROW_NG + 1], in1=ogc[:, 1 - par], op0=ALU.mult, op1=ALU.mult))
                    signal_b.close()
                if i is not None:
                    signal.close()
            attention_steps(dve, step)

            dve.wait_ge(y4_loaded, 16)
            for t in range(1, CT):
                if t > 1:
                    dve.wait_ge(ln_added, t - 1)
                dve.tensor_tensor(ln_f[:, 0, :], y4[:, 0, :] if t == 1 else ln_f[:, 0, :], y4[:, t, :], ALU.add
                                  ).then_inc(ln_added, 1)
            dve.wait_ge(ggb_pe, 1)
            dve.tensor_copy(ggb[:, :], pair[3][:, :]).then_inc(ggb_ready, 1)
            dve.wait_ge(ln_pe, 1)

            def centre(t):
                dve.scalar_tensor_tensor(out=y4[:, t, :], in0=pair[0][:, :], scalar=-1.0 / (CT * P), in1=y4[:, t, :],
                                         op0=ALU.mult, op1=ALU.add).then_inc(ln_dve, 1)

            def add_square(t):
                dve.wait_ge(ln_act, t + 1)
                if t > 1:
                    dve.wait_ge(ln_added, CT + t - 2)
                dve.tensor_tensor(ln_f[:, 1, :], ln_sq[:, 0, :] if t == 1 else ln_f[:, 1, :], ln_sq[:, t % 2, :], ALU.add
                                  ).then_inc(ln_added, 1)
            for t in range(CT - 1):
                centre(t)
            add_square(1)
            centre(CT - 1)
            for t in range(2, CT):
                add_square(t)
            dve.wait_ge(ln_act, CT + 1)

            def ln_lo(t):
                dve.wait_ge(ln_act, CT + 1 + 2 * (t + 1))
                dve.tensor_tensor(ha_lo[:, t, :], ln_f[:, t % 2, :], ha_hi[:, t, :], ALU.subtract).then_inc(ln_dve, 1)
            for t in range(CT):
                dve.tensor_tensor(y4[:, t, :], y4[:, t, :], ln_rs[:, :], ALU.mult).then_inc(ln_dve, 1)
                if t:
                    ln_lo(t - 1)
            ln_lo(CT - 1)

            def scaled_product(i, src, slot, count):
                dve.wait_ge(tail_ss, count)
                me.done(dve.reciprocal(rs[:, 1, i:i + 1], rs[:, 1, i:i + 1]))
                me.wait()
                dve.scalar_tensor_tensor(out=tail_tmp[:, slot, :], in0=src, scalar=rs[:, 1, i:i + 1], in1=ggb[:, :],
                                         op0=ALU.mult, op1=ALU.mult).then_inc(tail_read, 1)

            def residual(i):
                scaled_product(i, out_pair(i)[:, :], 1, i + 1)
                dve.wait_ge(tail_read, i + 1)
                dve.wait_ge(x1_loaded[i // 2], 16)
                dve.tensor_tensor(x1[:, i, :], x1[:, i, :], tail_tmp[:, 1, :], ALU.add).then_inc(tail_done, 1)

            def next_norm(i):
                dve.wait_ge(x1_ss, i + 1)
                if i >= 4:
                    dve.wait_ge(turned, 16 + 8)
                normalise(xs[:, i % 4, :], x1[:, i, :], i, 3).then_inc(xs_ready, 1)
            for i in range(TT):
                residual(i)
                if i in (4, 5):
                    modulate(1, full1, range(4 * (i - 4), 4 * (i - 3)))
                if i != 4:
                    for n in (4, 5) if i == 5 else (i,):
                        next_norm(n)
            modulate(1, full1, range(8, 16))


            def u_full(e, used, first=False):
                dve.wait_ge(gate_silu, e + 1)
                dve.wait_ge(w_used, used)
                if not first:
                    dve.wait_ge(u_ready, e)
                dve.tensor_tensor(ufull[:, :], gate[:, :], pair[1][:, :], ALU.mult).then_inc(ufull_ready, 1)

            def u_low(e, slot):
                dve.wait_ge(uhi_ready, e + 1)
                dve.tensor_tensor(u_lo[:, slot, :], ufull[:, :], u_hi[:, slot, :], ALU.subtract).then_inc(u_ready, 1)

            def add_tile(bk, i, used):
                if i < TT - 1:
                    dve.wait_ge(down_ready, bk * (TT - 1) + (i + 1))
                else:
                    dve.wait_ge(w_used, used)
                dve.tensor_tensor(yt[:, i, :], yt[:, i, :], pair[2 + i % 2][:, :], ALU.add).then_inc(y_added, 1)

            def add_down(bk, used):
                for i in range(TT):
                    add_tile(bk, i, used)
            F0 = N_IN + N_OUT
            u_full(0, F0 + 2, first=True)
            u_low(0, 0)
            dve.wait_ge(yt_zero, 1)
            with dve.Fori(0, FB - 1) as bk:
                u_full(bk * 2 + 1, bk * 6 + (F0 + 4))
                u_low(bk * 2 + 1, 1)
                u_full(bk * 2 + 2, bk * 6 + (F0 + 6))
                add_down(bk, bk * 6 + (F0 + 8))
                u_low(bk * 2 + 2, 0)
            u_full(FFT - 1, 6 * (FB - 1) + F0 + 4)
            u_low(FFT - 1, 1)
            dve.wait_ge(ggb_pe, 2)
            dve.tensor_copy(ggb[:, :], pair[0][:, :]).then_inc(ggb_ready, 1)
            dve.wait_ge(ggb_ready, 2)
            for i in range(TT + 1):
                if i < TT:
                    add_tile(FB - 1, i, 6 * (FB - 1) + F0 + 6)
                if i:
                    scaled_product(i - 1, yt[:, i - 1, :], (i - 1) % 2, TT + i)
            dve.wait_ge(tail_read, 2 * TT)
            dve.tensor_tensor(x1[:, TT - 1, :], x1[:, TT - 1, :], tail_tmp[:, (TT - 1) % 2, :], ALU.add
                              ).then_inc(last_done, 1)

        @block.tensor
        def _(pe):
            pe.wait_ge(consts_ready, 2)
            pe.wait_ge(vec_loaded, 16 * VEC_LOADS)
            pe.transpose(pair[3][:, 0:ROWS], rows_a[:, :], ident[0:ROWS, 0:ROWS])
            pe.transpose(pair[3][:, P:P + TAPS * CT], rows_b[:, :], ident[0:TAPS * CT, 0:TAPS * CT]).then_inc(vec_turned, 1)

            def column_sums(src, dst, tiles):
                for n in range(tiles):
                    i_ = pe.matmul(dst[:, n:n + 1], src[:, n * P:(n + 1) * P], ones[:, 0:1], start=True, stop=True)
                return i_
            pe.wait_ge(ada0_used, KT)
            pe.wait_ge(vec_ready, 2)
            column_sums(acc0, pair[3][:, 256:272], 16).then_inc(mod0_summed, 1)

            def turn_tiles(call, src, groups):
                for g in groups:
                    kt, half = turn_group(g)
                    if g >= 4:
                        pe.wait_ge(*modulated(call, g - 4))
                    for i in range(4):
                        tile = 4 * half + i
                        pe.wait_ge(xs_ready, TT * call + tile + 1)
                        i_ = pe.transpose(bank(4 * call + g % 4)[:, i * P:(i + 1) * P],
                                          src[:, tile % src.shape[1], kt * P:(kt + 1) * P], ident[:, :])
                    i_.then_inc(turned, 1)
            turn_tiles(0, x0, range(16))

            def split_product(dst, slot, w_cols, x_hi, x_lo, first, last):
                wh, wl = w_hi[:, slot, w_cols], w_lo[:, slot, w_cols]
                steps = [(wh, x_hi), (wh, x_lo), (wl, x_hi)]
                for s_, (w, x) in enumerate(steps):
                    for half in range(2):
                        cols = slice(half * HALF, (half + 1) * HALF)
                        i_ = pe.matmul(dst[:, cols], w, x[:, cols], start=first and s_ == 0, stop=last and s_ == 2)
                return i_

            def project(dst, slot):
                for kt in range(KT):
                    hi, lo = (ha_hi, ha_lo) if kt < 4 else (hb_hi, hb_lo)
                    i_ = split_product(dst, slot, slice(kt * P, (kt + 1) * P), hi[:, kt % 4, :], lo[:, kt % 4, :],
                                       kt == 0, kt == KT - 1)
                return i_

            pe.wait_ge(h_ready, 16)
            with pe.Fori(0, 4) as t:
                free = [(og_evac, t + CREDIT), (vt_evac, t + CREDIT), (gate_sig, t + 1), (u_evac, t + 1 + CREDIT),
                        (z_evac, t + 1), (q_evac, t + 1)]
                for j in range(6):
                    pe.wait_ge(w_split, t * 6 + (j + 1))
                    pe.wait_ge(*free[j])
                    project(pair[j % 2], j % WS).then_inc(w_used, 1)
                    if j == 2:
                        pe.wait_ge(ada_used, t * KT + KT + CREDIT)
                        pe.wait_ge(modt_ready, t + CREDIT)
                        column_sums(acc, pair[3][:, 288:288 + KT], KT).then_inc(modt_summed, 1)
                pe.wait_ge(vt_evac, t + 1 + CREDIT)
                pe.wait_ge(v_ready, t + CREDIT)
                for c in range(TT):
                    i_ = pe.transpose(pair[2][:, c * P:(c + 1) * P], vt[:, c * P:(c + 1) * P], ident[:, :])
                i_.then_inc(v_turned, 1)

            pe.wait_ge(modt_ready, 4 + CREDIT)
            pe.wait_ge(v_ready, 4 + CREDIT)

            def step(i, back, par):
                def on_front(s_, name):
                    pe.wait_ge(*event(s_, i, name))
                first = isinstance(i, int) and i == 0
                signal = Signals(at_pe_f)
                signal_b = Signals(at_pe_b)

                def scores(n):
                    if i is None:
                        return
                    on_front(at_dve_f, f"X{n}")
                    if n >= 3:
                        on_front(at_dve_f, "PD" if n == 3 else f"P{n - 4}")
                    elif n < 2 and not first:
                        pe.wait_ge(*event(at_dve_f, i - 1, f"P{n + 4}"))
                    for h in range(HEADS):
                        i_ = pe.matmul(score_bank(n)[:, h * P:(h + 1) * P], xr[:, n % 3, h, :], xr[:, n % 3, h, :],
                                       start=True, stop=True)
                    signal(f"S{n}", i_)
                if i is not None:
                    on_front(at_act_f, "KC")
                    if not first:
                        pe.wait_ge(*event(at_dve_f, i - 1, "P3"))
                    for h in range(HEADS):
                        i_ = pe.matmul(score_bank(-1)[:, h * P:(h + 1) * P], kc[:, h, :], q[:, h, ds(i * P, P)],
                                       start=True, stop=True)
                    signal("DIAG", i_)
                scores(0)
                scores(1)
                scores(2)
                if back is not None:
                    bp = 1 - par
                    pe.wait_ge(*event(at_pool_f, back, "QE"))
                    pe.wait_ge(*event(at_dve_f, back, "P5"))
                    for h in range(HEADS):
                        o = bank(5)[:, h * P:(h + 1) * P]
                        pe.matmul(o, pmat[:, bp, h, :], vc[:, bp, h, :], start=True, stop=False, skip_group_check=True)
                        for j in range(2):
                            rows = slice(j * CHUNK, (j + 1) * CHUNK)
                            i_ = pe.matmul(o[rows, :], qe[:, bp, h, rows], state[:, 2 * bp + j, h, :], start=False,
                                           stop=True, skip_group_check=True)
                    signal_b("O", i_)
                if i is not None:
                    on_front(at_pool_f, "KD")
                    if back is not None and not (isinstance(back, int) and back == 0):
                        pe.wait_ge(*event(at_dve_b, back - 1, "MIX"))
                    for h in range(HEADS):
                        i_ = pe.transpose(bank(2)[:, h * P:(h + 1) * P], kd[:, h, :], ident[:, :])
                    signal("KDT", i_)
                scores(3)
                scores(4)
                if i is not None:
                    on_front(at_act_f, "KDT")
                    for j in range(2):
                        rows = slice(j * CHUNK, (j + 1) * CHUNK)
                        for h in range(HEADS):
                            i_ = pe.matmul(bank(3 + j)[:, h * P:(h + 1) * P], kdt[rows, h, :], vc[rows, par, h, :],
                                           start=True, stop=True)
                        signal(f"C{j}", i_)
                scores(5)
                if back is not None:
                    turn_output(back, signal_b)
                if i is not None:
                    signal.close()

            def turn_output(back, signal_b):
                pe.wait_ge(*event(at_dve_b, back, "ON"))
                for h in range(HEADS):
                    i_ = pe.transpose(bank(2)[:, h * P:(h + 1) * P], on[:, h, :], ident[:, :])
                signal_b("OT", i_)
                signal_b.close()
            attention_steps(pe, step)

            def gg_rows(call, dst):
                for n in range(KT):
                    i_ = pe.matmul(dst[:, n * P:(n + 1) * P], gg[:, call, n:n + 1].to_broadcast([P, P]), ident[:, :],
                                   start=True, stop=True)
                i_.then_inc(ggb_pe, 1)
            pe.wait_ge(mod_ready, 4)
            pe.wait_ge(*event(at_pool_b, TT - 1, "LO"))
            gg_rows(0, pair[3])

            def token_product(dst, x_hi, x_lo, wh, wl, first, last):
                for s_, (x, w) in enumerate([(x_hi, wh), (x_hi, wl), (x_lo, wh)]):
                    for half in range(2):
                        cols = slice(half * HALF, (half + 1) * HALF)
                        i_ = pe.matmul(dst[:, cols], x, w[:, cols], start=first and s_ == 0, stop=last and s_ == 2)
                return i_

            def out_tile(i, steps):
                tokens = slice(i * P, (i + 1) * P)
                for n in steps:
                    if i == 0:
                        pe.wait_ge(w_split, N_IN + n + 1)
                        if n >= 4:
                            pe.wait_ge(ln_dve, CT + min(2 * (n - 4) + 3, 2 * CT))
                    kt = OUT_K[n]
                    hi, lo = (ha_hi, ha_lo) if kt < 4 else (hb_hi, hb_lo)
                    g = N_IN + n
                    wh, wl = ((w_hi[:, g % WS, :], w_lo[:, g % WS, :]) if n < WS else
                              (wo_hi[:, n - WS, :], wo_lo[:, n - WS, :]))
                    i_ = token_product(out_pair(i), hi[:, kt % 4, tokens], lo[:, kt % 4, tokens], wh, wl,
                                       n == 0, n == N_OUT - 1)
                return i_

            def channel_sums(dst, src):
                for half in range(2):
                    cols = slice(half * HALF, (half + 1) * HALF)
                    i_ = pe.matmul(dst[:, cols], ones[:, :], src[:, cols], start=True, stop=True)
                i_.then_inc(ln_pe, 1)
            pe.wait_ge(ln_added, CT - 1)
            channel_sums(pair[0], ln_f[:, 0, :])
            out_tile(0, range(4))
            pe.wait_ge(ggb_ready, 1)
            out_tile(1, range(4))
            pe.wait_ge(ln_added, 2 * (CT - 1))
            channel_sums(pair[1], ln_f[:, 1, :])

            out_tile(2, range(4))
            pe.wait_ge(ln_act, CT + 1)
            out_tile(3, range(4))
            for i in range(TT - 2):
                if i >= 4:
                    pe.wait_ge(tail_read, i - 1)
                out_tile(i, range(4 if i < 4 else 0, N_OUT)).then_inc(w_used, 1)
                if i in (4, 5):
                    turn_tiles(1, xs, range(4 * (i - 4), 4 * (i - 3)))
            for i in (TT - 2, TT - 1):
                pe.wait_ge(tail_read, i - 1)
                i_ = out_tile(i, range(WS))
            i_.then_inc(ring_free, 1)
            for i in (TT - 2, TT - 1):
                out_tile(i, range(WS, N_OUT)).then_inc(w_used, 1)

            pe.wait_ge(h_ready, 16 + 8)
            F0 = N_IN + N_OUT

            def project_half(dst, slot, half):
                cols = slice(half * HALF, (half + 1) * HALF)
                for kt in range(KT):
                    hi, lo = (ha_hi, ha_lo) if kt < 4 else (hb_hi, hb_lo)
                    w = slice(kt * P, (kt + 1) * P)
                    wh, wl = w_hi[:, slot, w], w_lo[:, slot, w]
                    for s_, (a, x) in enumerate([(wh, hi), (wh, lo), (wl, hi)]):
                        i_ = pe.matmul(dst[:, cols], a, x[:, kt % 4, cols], start=kt == 0 and s_ == 0,
                                       stop=kt == KT - 1 and s_ == 2)
                return i_

            def gate_up(e, need, slot):
                pe.wait_ge(w_split, need + 1)
                pe.wait_ge(gate_silu, e)
                project(pair[0], slot % WS).then_inc(w_used, 1)
                pe.wait_ge(w_split, need + 2)
                pe.wait_ge(ufull_ready, e)
                project(pair[1], (slot + 1) % WS).then_inc(w_used, 1)

            def down(bk, need, slot):
                pe.wait_ge(w_split, need + 2)
                pe.wait_ge(u_ready, bk * 2 + 2)
                for i in range(TT):
                    pe.wait_ge(y_added, bk * TT + max(0, i - 1) + CREDIT)
                    tokens = slice(i * P, (i + 1) * P)
                    for f in range(2):
                        i_ = token_product(pair[2 + i % 2], u_hi[:, f, tokens], u_lo[:, f, tokens],
                                           w_hi[:, (slot + f) % WS, :], w_lo[:, (slot + f) % WS, :], f == 0, f == 1)
                    if i < TT - 1:
                        i_.then_inc(down_ready, 1)
                    else:
                        i_.then_inc(w_used, 2)
            for half in range(2):
                for n in range(2):
                    if half == 0:
                        pe.wait_ge(w_split, F0 + n + 1)
                        pe.wait_ge(tail_read, TT - 1 + n)
                    elif n == 0:
                        pe.wait_ge(h_ready, 32)
                    i_ = project_half(pair[n], (F0 + n) % WS, half)
                    if half:
                        i_.then_inc(w_used, 1)
                    else:
                        turn_tiles(1, xs, range(8 + 4 * n, 12 + 4 * n))
            with pe.Fori(0, FB - 1) as bk:
                gate_up(bk * 2 + 1, bk * 6 + (F0 + 2), F0 + 2)
                gate_up(bk * 2 + 2, bk * 6 + (F0 + 4), F0 + 4)
                down(bk, bk * 6 + (F0 + 6), F0 + 6)
            gate_up(FFT - 1, 6 * (FB - 1) + F0 + 2, F0 + 2)
            pe.wait_ge(ufull_ready, FFT)
            gg_rows(1, pair[0])
            down(FB - 1, 6 * (FB - 1) + F0 + 4, F0 + 4)


_SHAPES = [("x", (1, S, D)), ("c", (1, D)), ("w_ada", (1, D, 6 * D)), ("b_ada", (1, 6 * D)), ("g_pre_mix", (1, D)),
           ("g_post_mix", (1, D)), ("w_in", (1, D, 3 * D)), ("conv_w", (1, TAPS, CT * P)), ("conv_b", (1, CT * P)),
           ("conv_ln_g", (1, CT * P)), ("conv_ln_b", (1, CT * P)), ("hgrn_lower_bounds", (1, HEADS * P)),
           ("hgrn_norm_g", (1, P)), ("w_out", (1, D, D)), ("g_pre_ffn", (1, D)), ("g_post_ffn", (1, D)),
           ("w_ffn_in", (1, D, 2 * D_FF)), ("w_ffn_out", (1, D_FF, D))]


def kernel(**inputs):
    import numpy as np
    import concourse.bacc as bacc
    from concourse.bass_utils import run_bass_kernel_spmd

    nc = bacc.Bacc("TRN2", target_bir_lowering=False, num_devices=1)
    arrays, t_in = {}, {}
    for name, shape in _SHAPES:
        a = np.ascontiguousarray(inputs[name])
        assert a.shape == shape, (name, a.shape)
        arrays[f"in_{name}"] = a
        t_in[name] = nc.dram_tensor(f"in_{name}", a.shape, mybir.dt.from_np(a.dtype), kind="ExternalInput").ap()
    out = nc.dram_tensor("out", (1, S, D), F32, kind="ExternalOutput").ap()
    build(nc, t_in, out)
    result = run_bass_kernel_spmd(nc, [arrays], core_ids=[0])
    return result.results[0]["out"]
```
